# Optimizing a Trainium2 kernel written in Bass

```python
import math
import jax
import jax.numpy as jnp
from jax import lax
import numpy as np
import jax, jax.numpy as jnp

D_MODEL = 1024
BATCH = 1
SEQ = 256
DEPTH = 1

GRID_W = 64
CTX_LEN = 256

DA_HEADS = 4
DA_HEAD_DIM = 64
DA_V_DIM = 2 * DA_HEAD_DIM
DA_WIDTH = DA_HEADS * DA_V_DIM
HG_HEADS = 4
HG_HEAD_DIM = 128
HG_WIDTH = HG_HEADS * HG_HEAD_DIM
MIX_WIDTH = DA_WIDTH + HG_WIDTH
IN_WIDTH = 3 * DA_WIDTH + 5 * HG_WIDTH
SPLITS = (DA_WIDTH, 2 * DA_WIDTH, 3 * DA_WIDTH, 3 * DA_WIDTH + HG_WIDTH,
          3 * DA_WIDTH + 2 * HG_WIDTH, 3 * DA_WIDTH + 3 * HG_WIDTH, 3 * DA_WIDTH + 4 * HG_WIDTH)
CTX_KV_END = 3 * DA_WIDTH + 3 * HG_WIDTH
CTX_SPLITS = (DA_WIDTH, 2 * DA_WIDTH, 2 * DA_WIDTH + HG_WIDTH, 2 * DA_WIDTH + 2 * HG_WIDTH)
CHUNK = 64
Q_BLOCK = 128
N_EXPERTS = 16
CAPACITY_FACTOR = 2
EXPERT_FF = 1024
ROPE_THETA = 10000.0
NORM_EPS = 1e-6


def rmsnorm(x, g):
    xf = x.astype(jnp.float32)
    y = xf * lax.rsqrt(jnp.mean(xf * xf, axis=-1, keepdims=True) + NORM_EPS)
    return (y * g.astype(jnp.float32)).astype(x.dtype)

def modulate(h, shift, scale):
    return h * (1.0 + scale) + shift

def axial_rope_tables(rows):
    half = DA_HEAD_DIM // 2
    inv_freq = 1.0 / (ROPE_THETA ** (jnp.arange(0, half, 2, dtype=jnp.float32) / half))
    r, col = jnp.meshgrid(jnp.arange(rows, dtype=jnp.float32),
                          jnp.arange(GRID_W, dtype=jnp.float32), indexing="ij")
    ang_r = r.reshape(-1)[:, None] * inv_freq
    ang_c = col.reshape(-1)[:, None] * inv_freq
    ang = jnp.concatenate([ang_r, ang_r, ang_c, ang_c], axis=-1)
    return jnp.cos(ang), jnp.sin(ang)

def apply_axial_rope(x, cos, sin):
    xf = x.astype(jnp.float32)
    x1, x2, x3, x4 = jnp.split(xf, 4, axis=-1)
    rot = jnp.concatenate([-x2, x1, -x4, x3], axis=-1)
    return (xf * cos + rot * sin).astype(x.dtype)

def qk_heads(a):
    b, t = a.shape[:2]
    return a.reshape(b, t, DA_HEADS, 2, DA_HEAD_DIM).transpose(0, 2, 3, 1, 4)

def to_heads(a, n_heads, dim):
    b, t = a.shape[:2]
    return a.reshape(b, t, n_heads, dim).transpose(0, 2, 1, 3)

def merge_heads(o):
    b, h, t, d = o.shape
    return o.transpose(0, 2, 1, 3).reshape(b, t, h * d)

def diff_attend(q, k, v, lam):
    s = jnp.einsum("bhiqd,bhikd->bhiqk", q, k).astype(jnp.float32) * (DA_HEAD_DIM ** -0.5)
    p = jax.nn.softmax(s, axis=-1)
    a = p[:, :, 0] - lam * p[:, :, 1]
    return jnp.einsum("bhqk,bhkd->bhqd", a.astype(v.dtype), v)

def hgrn2_chunk_scan(k, v, log_f, s0, q=None):
    b_, h_, t_, _ = k.shape
    dv = v.shape[-1]
    n = t_ // CHUNK

    def chunks(a):
        return jnp.moveaxis(a.astype(jnp.float32).reshape(b_, h_, n, CHUNK, a.shape[-1]), 2, 0)

    lower = jnp.tril(jnp.ones((CHUNK, CHUNK), dtype=bool))[:, :, None]

    def step(S, inp):
        kc, vc, lc = inp[0], inp[1], inp[2]
        bcum = jnp.cumsum(lc, axis=2)
        b_end = bcum[:, :, -1:, :]
        S_next = (jnp.exp(b_end[:, :, 0, :, None]) * S
                  + jnp.einsum("bhsk,bhsv->bhkv", kc * jnp.exp(b_end - bcum), vc))
        if q is None:
            return S_next, None
        qc = inp[3]
        rel = bcum[:, :, :, None, :] - bcum[:, :, None, :, :]
        decay = jnp.exp(jnp.where(lower, rel, -jnp.inf))
        scores = jnp.einsum("bhrk,bhsk,bhrsk->bhrs", qc, kc, decay)
        o = (jnp.einsum("bhrk,bhkv->bhrv", qc * jnp.exp(bcum), S)
             + jnp.einsum("bhrs,bhsv->bhrv", scores, vc))
        return S_next, o

    xs = (chunks(k), chunks(v), chunks(log_f))
    if q is not None:
        xs = xs + (chunks(q),)
    S_fin, o = lax.scan(step, s0, xs)
    if q is not None:
        o = jnp.moveaxis(o, 0, 2).reshape(b_, h_, t_, dv).astype(v.dtype)
    return o, S_fin

def forget_gate(z, lb):
    f = lb + (1.0 - lb) * jax.nn.sigmoid(z.astype(jnp.float32))
    return jnp.log(f), 1.0 - f

def token_mixer(h_lat, h_ctx, w_in, w_out, lam, lambda_init, da_subln, lb, hg_norm, cos, sin, ctx_out):
    b_ = h_lat.shape[0]
    da_q, da_k, da_v, hg_ff, hg_fb, hg_i, hg_q, hg_g = jnp.split(h_lat @ w_in, SPLITS, axis=-1)
    c_da_k, c_da_v, c_ff, c_fb, c_i = jnp.split(h_ctx @ w_in[:, DA_WIDTH:CTX_KV_END], CTX_SPLITS, axis=-1)
    if ctx_out:
        c_da_q = h_ctx @ w_in[:, :DA_WIDTH]
        c_hg_q, c_hg_g = jnp.split(h_ctx @ w_in[:, CTX_KV_END:], 2, axis=-1)

    q = apply_axial_rope(qk_heads(da_q), cos, sin)
    k_ctx = qk_heads(c_da_k)
    k_all = jnp.concatenate([k_ctx, apply_axial_rope(qk_heads(da_k), cos, sin)], axis=3)
    v_ctx = to_heads(c_da_v, DA_HEADS, DA_V_DIM)
    v_all = jnp.concatenate([v_ctx, to_heads(da_v, DA_HEADS, DA_V_DIM)], axis=2)
    t_ = q.shape[3]
    n_blk = t_ // Q_BLOCK
    q_blocks = jnp.moveaxis(q.reshape(b_, DA_HEADS, 2, n_blk, Q_BLOCK, DA_HEAD_DIM), 3, 0)
    o_blocks = lax.map(lambda qb: diff_attend(qb, k_all, v_all, lam), q_blocks)
    o_da = jnp.moveaxis(o_blocks, 0, 2).reshape(b_, DA_HEADS, t_, DA_V_DIM)
    out_da = merge_heads(rmsnorm(o_da, da_subln) * (1.0 - lambda_init))

    v_lat = to_heads(hg_i, HG_HEADS, HG_HEAD_DIM)
    v_c = to_heads(c_i, HG_HEADS, HG_HEAD_DIM)
    q_lat = to_heads(hg_q, HG_HEADS, HG_HEAD_DIM)
    q_c = to_heads(c_hg_q, HG_HEADS, HG_HEAD_DIM) if ctx_out else None
    s0 = jnp.zeros((b_, HG_HEADS, HG_HEAD_DIM, HG_HEAD_DIM), jnp.float32)
    o_hg_lat = None
    o_hg_ctx = None
    for d, (z_lat, z_ctx) in enumerate(((hg_ff, c_ff), (hg_fb, c_fb))):
        flip = (lambda a: a) if d == 0 else (lambda a: jnp.flip(a, axis=2))
        lf_l, k_l = forget_gate(z_lat, lb[d])
        lf_c, k_c = forget_gate(z_ctx, lb[d])
        k_l, lf_l = to_heads(k_l, HG_HEADS, HG_HEAD_DIM), to_heads(lf_l, HG_HEADS, HG_HEAD_DIM)
        k_c, lf_c = to_heads(k_c, HG_HEADS, HG_HEAD_DIM), to_heads(lf_c, HG_HEADS, HG_HEAD_DIM)
        o_c, S_c = hgrn2_chunk_scan(flip(k_c), flip(v_c), flip(lf_c), s0,
                                    q=None if q_c is None else flip(q_c))
        o_l, _ = hgrn2_chunk_scan(flip(k_l), flip(v_lat), flip(lf_l), S_c, q=flip(q_lat))
        o_hg_lat = flip(o_l) if o_hg_lat is None else o_hg_lat + flip(o_l)
        if ctx_out:
            o_hg_ctx = flip(o_c) if o_hg_ctx is None else o_hg_ctx + flip(o_c)
    out_hg = merge_heads(rmsnorm(o_hg_lat, hg_norm)) * jax.nn.silu(hg_g)

    y_lat = jnp.concatenate([out_da, out_hg], axis=-1) @ w_out
    if not ctx_out:
        return y_lat, None
    o_c_da = diff_attend(qk_heads(c_da_q), k_ctx, v_ctx, lam)
    out_c_da = merge_heads(rmsnorm(o_c_da, da_subln) * (1.0 - lambda_init))
    out_c_hg = merge_heads(rmsnorm(o_hg_ctx, hg_norm)) * jax.nn.silu(c_hg_g)
    y_ctx = jnp.concatenate([out_c_da, out_c_hg], axis=-1) @ w_out
    return y_lat, y_ctx

def expert_choice_ffn(h, w_router, w_gate, w_up, w_down):
    b_, t_, d_ = h.shape
    cap = CAPACITY_FACTOR * t_ // N_EXPERTS
    aff = jax.nn.softmax(jnp.einsum("btd,de->bte", h, w_router).astype(jnp.float32), axis=-1)
    top_aff, top_idx = lax.top_k(jnp.swapaxes(aff, 1, 2), cap)
    xin = jax.vmap(lambda hb, ib: hb[ib])(h, top_idx)
    g = jnp.einsum("becd,edf->becf", xin, w_gate)
    u = jnp.einsum("becd,edf->becf", xin, w_up)
    y = jnp.einsum("becf,efd->becd", jax.nn.silu(g) * u, w_down) * top_aff[..., None].astype(h.dtype)
    return jax.vmap(lambda yb, ib: jnp.zeros((t_, d_), h.dtype).at[ib.reshape(-1)].add(yb.reshape(-1, d_)))(y, top_idx)

def first_inputs(seed: int = 0) -> dict:
    key = jax.random.key(seed)
    ks = jax.random.split(key, 24)
    D = D_MODEL

    def nrm(k, shape, scale):
        return jax.random.normal(k, shape, jnp.float32) * scale

    return {
        "x": nrm(ks[0], (BATCH, SEQ, D), 1.0),
        "c": nrm(ks[1], (BATCH, D), 1.0),
        "ctx": nrm(ks[2], (BATCH, CTX_LEN, D), 1.0),
        "c_ctx": nrm(ks[3], (D,), 1.0),
        "w_ada": nrm(ks[4], (DEPTH, D, 6 * D), 0.5 * D ** -0.5),
        "b_ada": nrm(ks[5], (DEPTH, 6 * D), 0.02),
        "norm_pre_mix": 1.0 + nrm(ks[6], (DEPTH, D), 0.05),
        "norm_post_mix": 1.0 + nrm(ks[7], (DEPTH, D), 0.05),
        "norm_pre_ffn": 1.0 + nrm(ks[8], (DEPTH, D), 0.05),
        "norm_post_ffn": 1.0 + nrm(ks[9], (DEPTH, D), 0.05),
        "w_in": nrm(ks[10], (DEPTH, D, IN_WIDTH), D ** -0.5),
        "da_lambda_q1": nrm(ks[11], (DEPTH, DA_HEAD_DIM), 0.1),
        "da_lambda_k1": nrm(ks[12], (DEPTH, DA_HEAD_DIM), 0.1),
        "da_lambda_q2": nrm(ks[13], (DEPTH, DA_HEAD_DIM), 0.1),
        "da_lambda_k2": nrm(ks[14], (DEPTH, DA_HEAD_DIM), 0.1),
        "da_subln": 1.0 + nrm(ks[15], (DEPTH, DA_V_DIM), 0.05),
        "hg_lower_bound": nrm(ks[16], (DEPTH + 1, 2, HG_WIDTH), 0.5),
        "hg_norm": 1.0 + nrm(ks[17], (DEPTH, HG_HEAD_DIM), 0.05),
        "w_out": nrm(ks[18], (DEPTH, MIX_WIDTH, D), MIX_WIDTH ** -0.5),
        "w_router": nrm(ks[19], (DEPTH, D, N_EXPERTS), D ** -0.5),
        "w_gate": nrm(ks[20], (DEPTH, N_EXPERTS, D, EXPERT_FF), D ** -0.5),
        "w_up": nrm(ks[21], (DEPTH, N_EXPERTS, D, EXPERT_FF), D ** -0.5),
        "w_down": nrm(ks[22], (DEPTH, N_EXPERTS, EXPERT_FF, D), EXPERT_FF ** -0.5),
    }

def first_block(x, c, ctx, c_ctx, w_ada, b_ada, norm_pre_mix, norm_post_mix, norm_pre_ffn, norm_post_ffn,
              w_in, da_lambda_q1, da_lambda_k1, da_lambda_q2, da_lambda_k2, da_subln, hg_lower_bound,
              hg_norm, w_out, w_router, w_gate, w_up, w_down):
    T = x.shape[1]
    ROWS = T // GRID_W
    cos, sin = axial_rope_tables(ROWS)
    lb_all = jnp.cumsum(jax.nn.softmax(hg_lower_bound.astype(jnp.float32), axis=0), axis=0)
    x_lat, x_ctx = x, ctx
    for l in range(DEPTH):
        last = l == DEPTH - 1
        lambda_init = 0.8 - 0.6 * math.exp(-0.3 * l)
        lam = (jnp.exp(jnp.sum(da_lambda_q1[l].astype(jnp.float32) * da_lambda_k1[l].astype(jnp.float32)))
               - jnp.exp(jnp.sum(da_lambda_q2[l].astype(jnp.float32) * da_lambda_k2[l].astype(jnp.float32)))
               + lambda_init)
        mod_lat = jax.nn.silu(c) @ w_ada[l] + b_ada[l]
        mod_ctx = jax.nn.silu(c_ctx) @ w_ada[l] + b_ada[l]
        sh1, sc1, gt1, sh2, sc2, gt2 = jnp.split(mod_lat[:, None, :], 6, axis=-1)
        csh1, csc1, cgt1, csh2, csc2, cgt2 = jnp.split(mod_ctx, 6, axis=-1)

        h_lat = modulate(rmsnorm(x_lat, norm_pre_mix[l]), sh1, sc1)
        h_ctx = modulate(rmsnorm(x_ctx, norm_pre_mix[l]), csh1, csc1)
        y_lat, y_ctx = token_mixer(h_lat, h_ctx, w_in[l], w_out[l], lam, lambda_init, da_subln[l],
                                   lb_all[l], hg_norm[l], cos, sin, not last)
        x_lat = x_lat + gt1 * rmsnorm(y_lat, norm_post_mix[l])
        h_lat = modulate(rmsnorm(x_lat, norm_pre_ffn[l]), sh2, sc2)
        f_lat = expert_choice_ffn(h_lat, w_router[l], w_gate[l], w_up[l], w_down[l])
        x_lat = x_lat + gt2 * rmsnorm(f_lat, norm_post_ffn[l])
        if not last:
            x_ctx = x_ctx + cgt1 * rmsnorm(y_ctx, norm_post_mix[l])
            h_ctx = modulate(rmsnorm(x_ctx, norm_pre_ffn[l]), csh2, csc2)
            f_ctx = expert_choice_ffn(h_ctx, w_router[l], w_gate[l], w_up[l], w_down[l])
            x_ctx = x_ctx + cgt2 * rmsnorm(f_ctx, norm_post_ffn[l])
    return x_lat


DEPTH_2 = 2

HEAD_DIM = 64
N_MEM = 256
MEM_HEADS = 4
CROSS_WIDTH = MEM_HEADS * HEAD_DIM
MIX_WIDTH_2 = 12 * HEAD_DIM
ATTN_WIDTH = MIX_WIDTH_2 + CROSS_WIDTH
EPS = 1e-6
NEG = -1e30
MLA_HEADS = 12
MLA_Q_RANK = 384
MLA_KV_RANK = 256
MLA_NOPE = 64
MLA_ROPE = 32
MLA_V = 64
MLA_QK = MLA_NOPE + MLA_ROPE
MLA_IN = MLA_Q_RANK + MLA_KV_RANK + MLA_ROPE + CROSS_WIDTH
SWA_Q_HEADS = 12
SWA_KV_HEADS = 4
SWA_GROUP = SWA_Q_HEADS // SWA_KV_HEADS
WINDOW = 128
SWA_IN = (SWA_Q_HEADS + 2 * SWA_KV_HEADS) * HEAD_DIM + CROSS_WIDTH
D_FF = 4 * D_MODEL
N_MLA_LAYERS = (DEPTH_2 + 1) // 2
N_SWA_LAYERS = DEPTH_2 // 2


def rmsnorm_2(x, g):
    xf = x.astype(jnp.float32)
    y = xf * lax.rsqrt(jnp.mean(xf * xf, axis=-1, keepdims=True) + EPS)
    return (y * g.astype(jnp.float32)).astype(x.dtype)

def rope(x, positions):
    r = x.shape[-1]
    half = r // 2
    inv = ROPE_THETA ** (-(jnp.arange(half, dtype=jnp.float32) * 2.0) / r)
    ang = positions.astype(jnp.float32)[..., None] * inv
    cos = jnp.cos(ang)[:, :, None, :]
    sin = jnp.sin(ang)[:, :, None, :]
    xf = x.astype(jnp.float32)
    x1, x2 = xf[..., :half], xf[..., half:]
    out = jnp.concatenate([x1 * cos - x2 * sin, x1 * sin + x2 * cos], axis=-1)
    return out.astype(x.dtype)

def alibi_slopes(n_heads):
    return 2.0 ** (-8.0 * (jnp.arange(n_heads, dtype=jnp.float32) + 1.0) / n_heads)

def causal_dense_attention(q, k, v):
    b, s, h, dk = q.shape
    dv = v.shape[-1]
    nb = s // Q_BLOCK
    scale = dk ** -0.5
    qb = q.reshape(b, nb, Q_BLOCK, h, dk).transpose(1, 0, 2, 3, 4)
    k_idx = jnp.arange(s)

    def one_block(args):
        q_blk, n = args
        t_idx = n * Q_BLOCK + jnp.arange(Q_BLOCK)
        sc = jnp.einsum('bqhd,bkhd->bhqk', q_blk, k,
                        preferred_element_type=jnp.float32) * scale
        mask = k_idx[None, :] <= t_idx[:, None]
        sc = jnp.where(mask[None, None], sc, NEG)
        p = jax.nn.softmax(sc, axis=-1).astype(v.dtype)
        return jnp.einsum('bhqk,bkhd->bqhd', p, v)

    out = lax.map(one_block, (qb, jnp.arange(nb)))
    return out.transpose(1, 0, 2, 3, 4).reshape(b, s, h, dv)

def mla_mixer(hn, positions, w_in, q_norm_g, kv_norm_g, w_uq, w_ukv):
    b, s, _ = hn.shape
    proj = hn @ w_in
    c_q = proj[..., :MLA_Q_RANK]
    c_kv = proj[..., MLA_Q_RANK:MLA_Q_RANK + MLA_KV_RANK]
    k_r = proj[..., MLA_Q_RANK + MLA_KV_RANK:MLA_Q_RANK + MLA_KV_RANK + MLA_ROPE]
    q_cross = proj[..., MLA_Q_RANK + MLA_KV_RANK + MLA_ROPE:]
    q = (rmsnorm_2(c_q, q_norm_g) @ w_uq).reshape(b, s, MLA_HEADS, MLA_QK)
    q = jnp.concatenate([q[..., :MLA_NOPE], rope(q[..., MLA_NOPE:], positions)], axis=-1)
    kv = (rmsnorm_2(c_kv, kv_norm_g) @ w_ukv).reshape(b, s, MLA_HEADS, MLA_NOPE + MLA_V)
    k_nope, v = kv[..., :MLA_NOPE], kv[..., MLA_NOPE:]
    k_rope = jnp.broadcast_to(rope(k_r[:, :, None, :], positions),
                              (b, s, MLA_HEADS, MLA_ROPE))
    k = jnp.concatenate([k_nope, k_rope], axis=-1)
    o = causal_dense_attention(q, k, v)
    return o.reshape(b, s, MLA_HEADS * MLA_V), q_cross

def _with_prev_block(a):
    pad = [(0, 0), (1, 0)] + [(0, 0)] * (a.ndim - 2)
    prev = jnp.pad(a[:, :-1], pad)
    return jnp.concatenate([prev, a], axis=2)

def swa_mixer(hn, positions, w_in, sinks):
    b, s, _ = hn.shape
    nb = s // WINDOW
    proj = hn @ w_in
    nq = SWA_Q_HEADS * HEAD_DIM
    nk = SWA_KV_HEADS * HEAD_DIM
    q = proj[..., :nq].reshape(b, nb, WINDOW, SWA_KV_HEADS, SWA_GROUP, HEAD_DIM)
    k = proj[..., nq:nq + nk].reshape(b, nb, WINDOW, SWA_KV_HEADS, HEAD_DIM)
    v = proj[..., nq + nk:nq + 2 * nk].reshape(b, nb, WINDOW, SWA_KV_HEADS, HEAD_DIM)
    q_cross = proj[..., nq + 2 * nk:]
    kk = _with_prev_block(k)
    vv = _with_prev_block(v)
    pos_q = positions.reshape(b, nb, WINDOW)
    pos_k = _with_prev_block(pos_q)
    sc = jnp.einsum('bnqhgd,bnkhd->bnhgqk', q, kk,
                    preferred_element_type=jnp.float32) * (HEAD_DIM ** -0.5)
    dist = (pos_q[..., :, None] - pos_k[..., None, :]).astype(jnp.float32)
    slopes = alibi_slopes(SWA_Q_HEADS).reshape(SWA_KV_HEADS, SWA_GROUP)
    sc = sc - slopes[None, None, :, :, None, None] * dist[:, :, None, None]
    qi = jnp.arange(WINDOW)[:, None]
    kj = jnp.arange(2 * WINDOW)[None, :]
    rel = WINDOW + qi - kj
    band = (rel >= 0) & (rel < WINDOW)
    valid = band[None] & ((jnp.arange(nb)[:, None, None] > 0) | (kj >= WINDOW)[None])
    sc = jnp.where(valid[None, :, None, None], sc, NEG)
    sink = sinks.astype(jnp.float32).reshape(SWA_KV_HEADS, SWA_GROUP)[None, None, :, :, None, None]
    sink = jnp.broadcast_to(sink, sc.shape[:-1] + (1,))
    p = jax.nn.softmax(jnp.concatenate([sc, sink], axis=-1), axis=-1)[..., :-1]
    o = jnp.einsum('bnhgqk,bnkhd->bnqhgd', p.astype(vv.dtype), vv)
    return o.reshape(b, s, SWA_Q_HEADS * HEAD_DIM), q_cross

def memory_cross_attention(q_cross, mem_n, w_mem_kv):
    b, s, _ = q_cross.shape
    kv = (mem_n @ w_mem_kv).reshape(b, N_MEM, 2, MEM_HEADS, HEAD_DIM)
    k, v = kv[:, :, 0], kv[:, :, 1]
    q = q_cross.reshape(b, s, MEM_HEADS, HEAD_DIM)
    sc = jnp.einsum('bshd,bmhd->bhsm', q, k,
                    preferred_element_type=jnp.float32) * (HEAD_DIM ** -0.5)
    p = jax.nn.softmax(sc, axis=-1).astype(v.dtype)
    return jnp.einsum('bhsm,bmhd->bshd', p, v).reshape(b, s, CROSS_WIDTH)

def squared_relu_mlp(h, w_up, w_down):
    a = jax.nn.relu(h @ w_up)
    return (a * a) @ w_down

def second_inputs(seed: int = 0) -> dict:
    key = jax.random.key(seed)
    ks = jax.random.split(key, 20)

    def w(k, shape, fan_in):
        return jax.random.normal(k, shape, jnp.float32) * (fan_in ** -0.5)

    def gain(k, shape):
        return 1.0 + 0.02 * jax.random.normal(k, shape, jnp.float32)

    x = jax.random.normal(ks[0], (BATCH, SEQ, D_MODEL), jnp.float32)
    mem = jax.random.normal(ks[1], (BATCH, N_MEM, D_MODEL), jnp.float32)
    offsets = jax.random.randint(ks[2], (BATCH, 1), 0, 1024, dtype=jnp.int32)
    positions = (offsets + jnp.arange(SEQ, dtype=jnp.int32)[None, :]).astype(jnp.int32)
    return {
        "x": x,
        "mem": mem,
        "positions": positions,
        "attn_norm_g": gain(ks[3], (DEPTH_2, D_MODEL)),
        "mlp_norm_g": gain(ks[4], (DEPTH_2, D_MODEL)),
        "mem_norm_g": gain(ks[5], (D_MODEL,)),
        "final_norm_g": gain(ks[6], (D_MODEL,)),
        "mla_w_in": w(ks[7], (N_MLA_LAYERS, D_MODEL, MLA_IN), D_MODEL),
        "mla_q_norm_g": gain(ks[8], (N_MLA_LAYERS, MLA_Q_RANK)),
        "mla_kv_norm_g": gain(ks[9], (N_MLA_LAYERS, MLA_KV_RANK)),
        "mla_w_uq": w(ks[10], (N_MLA_LAYERS, MLA_Q_RANK, MLA_HEADS * MLA_QK), MLA_Q_RANK),
        "mla_w_ukv": w(ks[11], (N_MLA_LAYERS, MLA_KV_RANK, MLA_HEADS * (MLA_NOPE + MLA_V)), MLA_KV_RANK),
        "swa_w_in": w(ks[12], (N_SWA_LAYERS, D_MODEL, SWA_IN), D_MODEL),
        "swa_sinks": 0.5 * jax.random.normal(ks[13], (N_SWA_LAYERS, SWA_Q_HEADS), jnp.float32),
        "w_mem_kv": w(ks[14], (DEPTH_2, D_MODEL, 2 * CROSS_WIDTH), D_MODEL),
        "w_o": w(ks[15], (DEPTH_2, ATTN_WIDTH, D_MODEL), ATTN_WIDTH),
        "mlp_w_up": w(ks[16], (DEPTH_2, D_MODEL, D_FF), D_MODEL),
        "mlp_w_down": w(ks[17], (DEPTH_2, D_FF, D_MODEL), D_FF),
    }

def second_block(x, mem, positions, attn_norm_g, mlp_norm_g, mem_norm_g, final_norm_g,
              mla_w_in, mla_q_norm_g, mla_kv_norm_g, mla_w_uq, mla_w_ukv,
              swa_w_in, swa_sinks, w_mem_kv, w_o, mlp_w_up, mlp_w_down):
    mem_n = rmsnorm_2(mem, mem_norm_g)
    for i in range(DEPTH_2):
        j = i // 2
        hn = rmsnorm_2(x, attn_norm_g[i])
        if i % 2 == 0:
            mix, q_cross = mla_mixer(hn, positions, mla_w_in[j], mla_q_norm_g[j],
                                     mla_kv_norm_g[j], mla_w_uq[j], mla_w_ukv[j])
        else:
            mix, q_cross = swa_mixer(hn, positions, swa_w_in[j], swa_sinks[j])
        cross = memory_cross_attention(q_cross, mem_n, w_mem_kv[i])
        x = x + jnp.concatenate([mix, cross], axis=-1) @ w_o[i]
        x = x + squared_relu_mlp(rmsnorm_2(x, mlp_norm_g[i]), mlp_w_up[i], mlp_w_down[i])
    return rmsnorm_2(x, final_norm_g)


def setup_inputs(seed=0):
    out = dict(first_inputs(seed))
    for name, value in second_inputs(seed + 1).items():
        if name != "x":
            out[name + "_2"] = value
    return out


def reference(
    x, c, ctx, c_ctx, w_ada, b_ada, norm_pre_mix, norm_post_mix, norm_pre_ffn, norm_post_ffn,
    w_in, da_lambda_q1, da_lambda_k1, da_lambda_q2, da_lambda_k2, da_subln, hg_lower_bound,
    hg_norm, w_out, w_router, w_gate, w_up, w_down, mem_2, positions_2, attn_norm_g_2,
    mlp_norm_g_2, mem_norm_g_2, final_norm_g_2, mla_w_in_2, mla_q_norm_g_2, mla_kv_norm_g_2,
    mla_w_uq_2, mla_w_ukv_2, swa_w_in_2, swa_sinks_2, w_mem_kv_2, w_o_2, mlp_w_up_2,
    mlp_w_down_2,
):
    x = first_block(
        x, c, ctx, c_ctx, w_ada, b_ada, norm_pre_mix, norm_post_mix, norm_pre_ffn,
        norm_post_ffn, w_in, da_lambda_q1, da_lambda_k1, da_lambda_q2, da_lambda_k2, da_subln,
        hg_lower_bound, hg_norm, w_out, w_router, w_gate, w_up, w_down,
    )
    return second_block(
        x, mem_2, positions_2, attn_norm_g_2, mlp_norm_g_2, mem_norm_g_2, final_norm_g_2,
        mla_w_in_2, mla_q_norm_g_2, mla_kv_norm_g_2, mla_w_uq_2, mla_w_ukv_2, swa_w_in_2,
        swa_sinks_2, w_mem_kv_2, w_o_2, mlp_w_up_2, mlp_w_down_2,
    )


_drawn_inputs = setup_inputs


def setup_inputs(seed=0):
    import zlib

    import numpy as np

    out = dict(_drawn_inputs(seed))
    spreads = {}
    factors = {'norm_post_ffn': 3.357,
     'da_lambda_k2': 3.18,
     'attn_norm_g_2': 6.326,
     'mem_norm_g_2': 8.0,
     'final_norm_g_2': 8.628,
     'mla_q_norm_g_2': 8.0,
     'mla_kv_norm_g_2': 8.0,
     'swa_sinks_2': 33.28,
     'mlp_norm_g_2': 3.216}
    for name, (base, spread) in spreads.items():
        noise = np.random.default_rng([zlib.crc32(name.encode()), seed]).standard_normal(out[name].shape)
        drawn = base * np.exp(spread * noise) if base else spread * noise
        out[name] = jnp.asarray(drawn.astype(out[name].dtype))
    for name, factor in factors.items():
        out[name] = (out[name] * factor).astype(out[name].dtype)
    return out
```

```python
from contextlib import ExitStack
from math import exp as _exp

import numpy as np
import concourse.bass as bass
from concourse import mybir

F32 = mybir.dt.float32
F32R = mybir.dt.float32r
I32 = mybir.dt.int32
U32 = mybir.dt.uint32
U8 = mybir.dt.uint8
ALU = mybir.AluOpType
ACT = mybir.ActivationFunctionType
AX = mybir.AxisListType.X

P = 128
D = 1024
KT = D // P
T = 256
TT = T // P
GW = 512
EPS = 1e-6
HEADS = 4
DH = 64
LEVELS = (64, 32, 16, 8, 4, 2, 1)
PRE, SUF = len(LEVELS), len(LEVELS) + 1
EXPERTS, CAP = 16, 32
GROUP = 4
NGROUPS = EXPERTS // GROUP
CHUNK = 4096
MLA_H, NOPE, ROPE, VD = 12, 64, 32, 64
QK = NOPE + ROPE
Q_RANK, KV_RANK = 384, 256
MLA_IN = Q_RANK + KV_RANK + ROPE + 256
CROSS_H = 4
KV_H = 4
LAMBDA_INIT = 0.8 - 0.6 * _exp(0.0)
TWO_PI = 2 * np.pi
MAGIC = 12582912.0

F_ADA, F_NPM, F_NPF, F_ATTN, F_MLP, F_MEM, F_QN, F_KVN = 0, 48, 56, 64, 80, 96, 104, 107
NFEAT = 109

C_ID, C_SEL, C_TOK, C_IOTA, C_MLA, C_SWA, C_COS, C_SIN, C_INV, C_EYE = 0, 128, 640, 642, 898, 1154, 1410, 1538, 1666, 1682
NCONST = C_EYE + EXPERTS * CAP
NEG = -1e30


def shape_tables():
    c = np.zeros((P, NCONST), np.float32)
    i = np.arange(P)
    c[i, C_ID + i] = 1.0
    for j in range(4):
        c[32 * j, C_SEL + 128 * j:C_SEL + 128 * (j + 1)] = 1.0
    c[:, C_TOK], c[:, C_TOK + 1] = i, i + P
    c[:, C_IOTA:C_IOTA + T] = np.arange(T)
    causal = np.where(i[None, :] <= i[:, None], 0.0, NEG)
    c[:, C_MLA + P:C_MLA + 2 * P] = causal
    c[:, C_SWA:C_SWA + P] = np.where(i[None, :] > i[:, None], 0.0, NEG)
    c[:, C_SWA + P:C_SWA + 2 * P] = causal
    inv = (1.0 / (np.float32(10000.0) ** (np.arange(0, 32, 2, dtype=np.float32) / np.float32(32)))).astype(np.float32)
    tok = np.arange(T)
    ang_r = (tok // 64).astype(np.float32)[:, None] * inv
    ang_c = (tok % 64).astype(np.float32)[:, None] * inv
    ang = np.concatenate([ang_r, ang_r, ang_c, ang_c], -1)
    sign = np.repeat(np.array([-1, 1, -1, 1], np.float32), 16)
    cos, sin = np.cos(ang), np.sin(ang) * sign
    for t in range(TT):
        c[:, C_COS + 64 * t:C_COS + 64 * (t + 1)] = cos[t * P:(t + 1) * P]
        c[:, C_SIN + 64 * t:C_SIN + 64 * (t + 1)] = sin[t * P:(t + 1) * P]
    c[:, C_INV:C_INV + 16] = np.float32(10000.0) ** (-(np.arange(16, dtype=np.float32) * np.float32(2.0)) / np.float32(ROPE))
    for e in range(EXPERTS):
        c[e, C_EYE + CAP * e:C_EYE + CAP * (e + 1)] = 1.0
    s, t = i[:, None], i[None, :]
    mov = np.zeros((P, 2, 9, P), np.float32)
    mask = np.zeros((P, 2, len(LEVELS), P), np.uint8)
    for d in range(2):
        upto = (s <= t) if d == 0 else (s >= t)
        after = ~upto
        for n, m in enumerate(LEVELS):
            late = ((t & m) > 0) == (d == 0)
            mov[:, d, n] = (s // m == t // m) & np.where(late, upto, after)
            mask[:, d, n] = (s // (2 * m) == t // (2 * m)) & (s // m != t // m) & ((s < t) if d == 0 else (s > t))
        mov[:, d, PRE], mov[:, d, SUF] = upto, after
    return {"tables": c, "decay_ops": mov.reshape(P, -1), "level_masks": mask.view(np.int32).reshape(P, -1)}


class Tally:

    def __init__(self, sem):
        self.sem, self.n = sem, 0

    def link(self, eng, ins):
        ins.then_inc(self.sem, 1)
        self.n += 1
        eng.wait_ge(self.sem, self.n)


def inverse_rms(dve, tally, ss, v, y, width, eps):
    tally.link(dve, dve.tensor_scalar(v, ss, 1.0 / width, eps, ALU.mult, ALU.add))
    tally.link(dve, dve.tensor_scalar(y.bitcast(I32), v.bitcast(I32), -0.5, 1597463007.0, ALU.mult, ALU.add))
    for _ in range(3):
        tally.link(dve, dve.scalar_tensor_tensor(ss, y, -0.5, y, ALU.mult, ALU.mult))
        tally.link(dve, dve.tensor_tensor(ss, ss, v, ALU.mult))
        tally.link(dve, dve.scalar_tensor_tensor(y, ss, 1.5, y, ALU.add, ALU.mult))


def program(nc, a, out):
    ctx = ExitStack()
    with ctx:
        body(nc, ctx, a, out)


def body(nc, ctx, a, out):
    def sb(name, shape, dt=F32, stack=ctx):
        return stack.enter_context(nc.sbuf_tensor(name, shape, dt))

    def sem(name):
        return ctx.enter_context(nc.semaphore(name))

    ps = ctx.enter_context(nc.psum_tensor("ps", [P, 8, GW], F32))

    cst = sb("cst", [P, NCONST])
    ones = sb("ones", [P, P])
    feat = sb("feat", [P, NFEAT])
    small = sb("small", [P, 64])
    xres = sb("xres", [P, TT, D])
    hT = sb("hT", [P, KT, T])
    mix = sb("mix", [P, TT, D])
    g2row = sb("g2row", [P, D])
    affA = sb("affA", [P, 2, 3, KT])
    subln = sb("subln", [P, 2, P])
    sinks = sb("sinks", [P, 12])
    lams = sb("lams", [P, 4, DH])
    posf = sb("posf", [P, TT])
    posrow = sb("posrow", [P, T])
    ring_lo = sb("ring_lo", [P, 3, CHUNK])

    ident = cst[:, C_ID:C_ID + P]
    dve_link = Tally(sem("dve_link"))
    loaded = [sem(f"slot_loaded{s}") for s in range(8)]
    ring_used = sem("ring_used")

    w_in = a["w_in"][0].rearrange("(k p) n -> p k n", p=P)
    w_ada = a["w_ada"][0].rearrange("(k p) n -> p k n", p=P)

    def rows(w, k0, k1, n0, n1):
        return w[0].rearrange("(k p) n -> p k n", p=P)[:, k0:k1, n0:n1]

    chunks = [w_ada[:, 2 * i:2 * i + 2, 0:2 * D] for i in range(4)]
    ADA1, WIN = 0, 4
    GROUP_ORDER = (3, 4, 5, 7, 6, 1, 0, 2)
    WITH_CTX = (1, 2, 3, 4, 5)
    chunks += [w_in[:, :, GW * g:GW * (g + 1)] for g in GROUP_ORDER]
    ADA2 = len(chunks)
    chunks += [w_ada[:, k:k + 1, 2 * D:6 * D] for k in range(KT)]
    WOUT = len(chunks)
    chunks += [rows(a["w_out"], 4 * i, 4 * i + 4, 0, D) for i in range(2)]
    MOE = len(chunks)
    moe_w = [a[n].rearrange("l (g e) (k p) n -> g k p (l e) n", e=GROUP, p=P) for n in ("w_gate", "w_up", "w_down")]

    def moe_chunk(g, c):
        w, k = (moe_w[c % 2], c // 2) if c < 16 else (moe_w[2], c - 16)
        if isinstance(g, int):
            return w[g, k]
        return w[bass.ds(g, 1), k].rearrange("g p e n -> p (g e) n")

    chunks += [moe_chunk(g, c) for g in range(NGROUPS) for c in range(24)]
    BLOCK2 = len(chunks)
    where = {}

    def add(name, parts):
        where[name] = len(chunks)
        chunks.extend(parts)

    def mem_chunk(l):
        return [a["w_mem_kv_2"][l].rearrange("(k p) n -> p k n", p=P)]

    add("mem0", mem_chunk(0))
    add("mla_in", [rows(a["mla_w_in_2"], 4 * i, 4 * i + 4, 0, MLA_IN) for i in range(2)])
    add("mem1", mem_chunk(1))
    add("uq", [a["mla_w_uq_2"][0].rearrange("(k p) n -> p k n", p=P)])
    add("ukv", [a["mla_w_ukv_2"][0].rearrange("(k p) n -> p k n", p=P)])

    def mlp_chunks(l):
        up = a["mlp_w_up_2"][l].rearrange("(k p) n -> p k n", p=P)
        down = a["mlp_w_down_2"][l].rearrange("(k p) n -> p k n", p=P)
        parts = []
        for i in range(9):
            if i < 8:
                parts.append(up[:, :, GW * i:GW * (i + 1)])
            if i > 0:
                parts.append(down[:, 4 * (i - 1):4 * i, :])
        return parts

    def wo_chunks(l):
        w = a["w_o_2"][l].rearrange("(k p) n -> p k n", p=P)
        return [w[:, 4 * i:4 * i + 4, :] for i in range(2)]

    add("wo0", wo_chunks(0))
    add("mlp0", mlp_chunks(0))
    add("swa_in", [a["swa_w_in_2"][0].rearrange("(k p) n -> p k n", p=P)[:, :, GW * i:GW * (i + 1)] for i in range(3)])
    add("wo1", wo_chunks(1))
    add("mlp1", mlp_chunks(1))

    def slot_of(n):
        if n < MOE:
            return n % (4 if ADA2 <= n < WOUT else 3)
        return (n - MOE) % 8 if n < BLOCK2 else (n - BLOCK2) % 3

    last_in, free_at, turn, count = {}, [], [], [0] * 8
    for n in range(len(chunks)):
        s = slot_of(n)
        free_at.append(last_in.get(s, -1) + 1)
        last_in[s] = n
        count[s] += 1
        turn.append(count[s])
    slots = [ring_lo[:, s, :] for s in range(3)] + [None] * 5
    issued = [0]

    def load_until(eng, end):
        for n in range(issued[0], end):
            if free_at[n]:
                eng.wait_ge(ring_used, free_at[n])
            src = chunks[n]
            k, w = src.shape[1], src.shape[2]
            eng.dma_start(slots[slot_of(n)][:, 0:k * w].rearrange("p (k w) -> p k w", k=k), src)\
               .then_inc(loaded[slot_of(n)], 16)
        issued[0] = max(issued[0], end)

    def loadable(read):
        n = issued[0]
        while n < len(chunks) and free_at[n] <= read and slots[slot_of(n)] is not None \
                and (n < MOE or slots[7] is not None or n >= BLOCK2):
            n += 1
        return n

    def chunk(eng, n, k):
        eng.wait_ge(loaded[slot_of(n)], 16 * turn[n])
        w = chunks[n].shape[2]
        return slots[slot_of(n)][:, 0:k * w].rearrange("p (k w) -> p k w", k=k)

    s_hi, s_lo, s_half = sem("upper_parts"), sem("lower_parts"), sem("first_half_read")
    turn_of = {}

    def register_split(*chunk_numbers):
        for n in chunk_numbers:
            turn_of[n] = len(turn_of)

    def half(buf, n, h):
        w = chunks[n].shape[1] * chunks[n].shape[2] // 2
        return buf[:, w * h:w * (h + 1)]

    def upper(act, w_hi, n, h):
        j = turn_of[n]
        act.wait_ge(loaded[slot_of(n)], 16 * turn[n])
        if j:
            if h == 0:
                act.wait_ge(s_half, j)
            else:
                act.wait_ge(ring_used, n)
        act.copy(half(w_hi, n, h).bitcast(F32R), half(slots[slot_of(n)], n, h)).then_inc(s_hi, 1)

    def lower(dve, w_hi, w_lo, n, h):
        x = half(slots[slot_of(n)], n, h)
        dve.wait_ge(s_hi, 2 * turn_of[n] + h + 1)
        dve.tensor_tensor(half(w_lo, n, h).bitcast(F32R), x, half(w_hi, n, h), ALU.subtract).then_inc(s_lo, 1)

    def split_chunk(pe, w_hi, w_lo, n):
        k, w = chunks[n].shape[1], chunks[n].shape[2]
        parts = [b[:, 0:k * w].bitcast(F32R).rearrange("p (k w) -> p k w", k=k) for b in (w_hi, w_lo)]
        return parts[0], parts[1], lambda h: pe.wait_ge(s_lo, 2 * turn_of[n] + h + 1)

    def product(pe, o, lhs, rhs, first, last):
        pe.matmul(o, lhs[0], rhs[0], start=first, stop=False)
        pe.matmul(o, lhs[0], rhs[1], start=False, stop=False)
        return pe.matmul(o, lhs[1], rhs[0], start=False, stop=last)

    mixer_stack = ctx.enter_context(ExitStack())

    def mb(name, shape, dt=F32, stack=mixer_stack):
        return sb(name, shape, dt, stack)

    s_in, s_x, s_late = sem("rows_loaded"), sem("x_loaded"), sem("late_loaded")
    g1row = mb("g1row", [P, D])
    mod_row2 = mb("mod_row2", [P, 2, GW])
    silu_c = mb("silu_c", [P, KT, 32])
    hcT = mb("hcT", [P, KT, T])

    def setup_stage():
        st = ExitStack()
        with st:
            ctxb = sb("ctxb", [P, TT, D], stack=st)
            xn = sb("xn_all", [P, 2 * TT, D], stack=st)
            junk = sb("junk", [P, D], stack=st)
            crow = sb("crow", [16, P], stack=st)
            frow = sb("frow", [NFEAT, P], stack=st)
            cT = sb("cT", [P, 16], stack=st)
            ce = sb("ce", [P, 16], stack=st)
            mod_row = sb("mod_row", [P, GW], stack=st)
            modT = sb("modT", [P, 2, 16], stack=st)
            posi = sb("posi", [P, TT], I32, stack=st)
            posri = sb("posri", [P, T], I32, stack=st)
            ss, rstd = small[:, 0:4], small[:, 4:8]
            s_vec, s_vecc, s_exp, s_cs, s_ada, s_row, s_modT, s_aff, s_ss, s_xn, s_xnp, s_xT = (sem(n) for n in (
                "vec_turned", "vec_copied", "exp_c", "silu_c_ready", "ada1_done", "mod_row_ready", "mod_turned",
                "affine_ready", "sum_squares", "xn_lat", "xn_ctx", "xn_turned"))
            s_one = sem("ones_ready")
            s_rstd = sem("rstd_ready")
            with nc.Block() as block:
                @block.sync
                def _(sp):
                    sp.dma_start(xres[:, :, :], a["x"][0].rearrange("(t p) d -> p t d", p=P)).then_inc(s_x, 16)
                    sp.dma_start(ctxb[:, :, :], a["ctx"][0].rearrange("(t p) d -> p t d", p=P)).then_inc(s_x, 16)
                    sp.wait_ge(s_in, 16 * ROWS)
                    load_until(sp, 4)
                    load_until(sp, loadable(4))

                @block.gpsimd
                def _(pool):
                    pool.memset(ones[:, :], 1.0).then_inc(s_one, 1)
                    pool.wait_ge(s_rstd, 1)
                    for t in range(TT):
                        xi = pool.tensor_scalar(xn[:, TT + t, :], ctxb[:, t, :], rstd[:, 2 + t:3 + t], None, ALU.mult)
                    xi.then_inc(s_xnp, 1)

                @block.scalar
                def _(act):
                    act.dma_start(crow[0:8, :], a["c"].rearrange("b (k p) -> (b k) p", p=P)).then_inc(s_in, 16)
                    act.dma_start(crow[8:16, :], a["c_ctx"].rearrange("(k p) -> k p", p=P)).then_inc(s_in, 16)
                    n = 2
                    for at, name, k in ((F_ADA, "b_ada", 48), (F_NPM, "norm_pre_mix", 8), (F_NPF, "norm_pre_ffn", 8),
                                        (F_ATTN, "attn_norm_g_2", 16), (F_MLP, "mlp_norm_g_2", 16),
                                        (F_QN, "mla_q_norm_g_2", 3), (F_KVN, "mla_kv_norm_g_2", 2)):
                        act.dma_start(frow[at:at + k, :], a[name].rearrange("l (k p) -> (l k) p", p=P)).then_inc(s_in, 16)
                        n += 1
                    act.dma_start(frow[F_MEM:F_MEM + 8, :], a["mem_norm_g_2"].rearrange("(k p) -> k p", p=P)).then_inc(s_in, 16)
                    act.dma_start(cst[:, :], a["tables"]).then_inc(s_in, 16)
                    assert n + 2 == ROWS
                    act.wait_ge(s_vecc, 1)
                    act.activation(ce[:, :], cT[:, :], ACT.Exp, scale=-1.0).then_inc(s_exp, 1)
                    act.dma_start(g1row[:, :], a["norm_post_mix"][0].partition_broadcast(P)).then_inc(s_late, 16)
                    act.dma_start(g2row[:, :], a["norm_post_ffn"][0].partition_broadcast(P)).then_inc(s_late, 16)
                    act.dma_start(subln[:, 0, :], a["da_subln"][0].partition_broadcast(P)).then_inc(s_late, 16)
                    act.dma_start(subln[:, 1, :], a["hg_norm"][0].partition_broadcast(P)).then_inc(s_late, 16)
                    act.dma_start(sinks[:, :], a["swa_sinks_2"][0].partition_broadcast(P)).then_inc(s_late, 16)
                    for i, name in enumerate(("da_lambda_q1", "da_lambda_k1", "da_lambda_q2", "da_lambda_k2")):
                        act.dma_start(lams[:, i, :], a[name][0].partition_broadcast(P)).then_inc(s_late, 16)
                    with nc.allow_non_contiguous_dma(reason="256 positions, one per partition"):
                        act.dma_start(posi[:, :], a["positions_2"][0].rearrange("(t p) -> p t", p=P)).then_inc(s_late, 16)
                    act.dma_start(posri[:, :], a["positions_2"][0].partition_broadcast(P)).then_inc(s_late, 16)
                    act.wait_ge(s_x, 32)
                    for j in range(4):
                        src = xres[:, j, :] if j < TT else ctxb[:, j - TT, :]
                        act.activation(junk[:, :], src, ACT.Square, accum_out=ss[:, j:j + 1]).then_inc(s_ss, 1)
                        act.wait_ge(s_ss, j + 1)
                    act.wait_ge(s_aff, 1)
                    for k in range(1, KT, 2):
                        act.wait_ge(s_xT, k + 1)
                        for r, dst in enumerate((hT, hcT)):
                            last = act.activation(dst[:, k, :], ps[:, 3 + k % 4, 256 * r:256 * (r + 1)], ACT.Identity,
                                                  scale=affA[:, r, 0, k:k + 1], bias=affA[:, r, 1, k:k + 1])
                        last.then_inc(s_evo, 1)

                @block.vector
                def _(dve):
                    dve_link.link(dve, dve.memset(silu_c[:, :, :], 0.0))
                    dve.wait_ge(s_vec, 1)
                    dve.tensor_copy(cT[:, :], ps[:, 0, 0:16])
                    dve.tensor_copy(feat[:, :], ps[:, 0, P:P + NFEAT]).then_inc(s_vecc, 1)
                    dve.wait_ge(s_exp, 1)
                    dve_link.link(dve, dve.tensor_scalar(ce[:, :], ce[:, :], 1.0, None, ALU.add))
                    dve_link.link(dve, dve.reciprocal(ce[:, :], ce[:, :]))
                    dve.tensor_tensor(silu_c[:, :, 0:2].rearrange("p k r -> p r k"), cT[:, :].rearrange("p (r k) -> p r k", r=2),
                                      ce[:, :].rearrange("p (r k) -> p r k", r=2), ALU.mult).then_inc(s_cs, 1)
                    dve.wait_ge(s_ss, 4)
                    inverse_rms(dve, dve_link, ss, small[:, 8:12], rstd, D, EPS)
                    dve.engine_nop().then_inc(s_rstd, 1)
                    for t in range(TT):
                        xi = dve.tensor_scalar(xn[:, t, :], xres[:, t, :], rstd[:, t:t + 1], None, ALU.mult)
                    xi.then_inc(s_xn, 1)
                    dve.wait_ge(s_ada, 1)
                    dve.tensor_copy(mod_row[:, :], ps[:, 1, :]).then_inc(s_row, 1)
                    dve.wait_ge(s_modT, 1)
                    for r in range(2):
                        last = dve.tensor_copy(modT[:, r, :].rearrange("p (j q) -> p j q", j=4),
                                               ps[:, 2, :].rearrange("p (q j s) -> p j q s", q=4, j=4)[:, :, :, r])
                    dve_link.link(dve, last)
                    for r in range(2):
                        dve.tensor_tensor(affA[:, r, 1, :], modT[:, r, 0:8], feat[:, F_ADA:F_ADA + 8], ALU.add)
                        dve_link.link(dve, dve.tensor_tensor(modT[:, r, 8:16], modT[:, r, 8:16], feat[:, F_ADA + 8:F_ADA + 16], ALU.add))
                        last = dve.scalar_tensor_tensor(affA[:, r, 0, :], modT[:, r, 8:16], 1.0, feat[:, F_NPM:F_NPM + 8], ALU.add, ALU.mult)
                    last.then_inc(s_aff, 1)
                    dve.wait_ge(s_aff, 1)
                    for k in range(0, KT, 2):
                        dve.wait_ge(s_xT, k + 1)
                        for r, dst in enumerate((hT, hcT)):
                            last = dve.tensor_scalar(dst[:, k, :], ps[:, 3 + k % 4, 256 * r:256 * (r + 1)],
                                                     affA[:, r, 0, k:k + 1], affA[:, r, 1, k:k + 1], ALU.mult, ALU.add)
                        last.then_inc(s_eve, 1)
                    dve.wait_ge(s_late, 16 * LATE)
                    dve.tensor_copy(posf[:, :], posi[:, :])
                    dve.tensor_copy(posrow[:, :], posri[:, :])

                @block.tensor
                def _(pe):
                    pe.wait_ge(s_in, 16 * ROWS)
                    pe.transpose(ps[:, 0, 0:16], crow[:, :], ident[0:16, 0:16])
                    pe.transpose(ps[:, 0, P:P + NFEAT], frow[:, :], ident[0:NFEAT, 0:NFEAT]).then_inc(s_vec, 1)
                    pe.wait_ge(s_cs, 1)
                    for k in range(KT):
                        w = chunk(pe, ADA1 + k // 2, 2)
                        for j in range(4):
                            mm = pe.matmul(ps[32 * j:32 * j + 32, 1, :], silu_c[:, k, :], w[:, k % 2, GW * j:GW * (j + 1)],
                                           start=(k == 0), stop=(k == KT - 1), skip_group_check=True)
                        if k % 2:
                            mm.then_inc(ring_used, 1)
                    mm2 = pe.transpose(ps[:, 2, 0:P], ident, ident)
                    mm2.then_inc(s_ada, 1)
                    pe.wait_ge(s_row, 1)
                    for q in range(4):
                        mm = pe.transpose(ps[:, 2, P * q:P * (q + 1)], mod_row[:, P * q:P * (q + 1)], ident)
                    mm.then_inc(s_modT, 1)
                    pe.wait_ge(s_xn, 1)
                    pe.wait_ge(s_xnp, 1)
                    for k in range(KT):
                        if k >= 4:
                            pe.wait_ge(s_evo if k % 2 else s_eve, k // 2 - 1)
                        for j in range(4):
                            mm = pe.transpose(ps[:, 3 + k % 4, P * j:P * (j + 1)], xn[:, j, P * k:P * (k + 1)], ident)
                        mm.then_inc(s_xT, 1)

    ROWS, LATE = 11, 11
    s_eve, s_evo = sem("hT_even"), sem("hT_odd")
    setup_stage()
    zl = mb("z_lat", [P, 8, TT, GW])
    zc = mb("z_ctx", [P, 5, TT, GW])

    def project_stage():
        st = ExitStack()
        with st:
            def rotate(eng, tally, x, t):
                cos = cst[:, C_COS + 64 * t:C_COS + 64 * (t + 1)]
                sin = cst[:, C_SIN + 64 * t:C_SIN + 64 * (t + 1)]

                xq, tq = (v.rearrange("p (h q c) -> p h q c", q=4, c=16) for v in (x, tmp[:, t, :]))
                sq = sin.rearrange("p (q c) -> p q c", c=16)
                for q in range(4):
                    last = eng.tensor_tensor(tq[:, :, q, :], xq[:, :, q ^ 1, :], sq[:, q:q + 1, :].to_broadcast([P, 8, 16]), ALU.mult)
                tally.link(eng, last)
                tally.link(eng, eng.tensor_tensor(x.rearrange("p (h c) -> p h c", c=64), x.rearrange("p (h c) -> p h c", c=64),
                                                  cos.unsqueeze(1).to_broadcast([P, 8, 64]), ALU.mult))
                return eng.tensor_tensor(x, x, tmp[:, t, :], ALU.add)

            tmp = mix[:, :, 0:GW]
            hTu, hTl, hcTu, hcTl = (sb(n, [P, KT, T], stack=st) for n in ("hT_u", "hT_l", "hcT_u", "hcT_l"))
            wq_hi, wq_lo = (sb(n, [P, 2, 2, GW], stack=st) for n in ("w_in_upper", "w_in_lower"))
            s_xu, s_xl, s_wu, s_wl, s_piece = (sem(n) for n in (
                "inputs_upper", "inputs_lower", "w_in_quarter_upper", "w_in_quarter_lower", "quarter_read"))

            def quarter(i, q):
                n = WIN + i
                return slots[slot_of(n)].rearrange("p (q k w) -> p q k w", q=4, k=2)[:, q]

            def upper_quarter(act, i, q):
                if q == 0:
                    act.wait_ge(loaded[slot_of(WIN + i)], 16 * turn[WIN + i])
                if q == 1 and i:
                    act.wait_ge(ring_used, WIN + i)
                elif q == 0 and i or q >= 2:
                    act.wait_ge(s_piece, 3 * i + max(q - 1, 0))
                act.copy(wq_hi[:, q % 2].bitcast(F32R), quarter(i, q)).then_inc(s_wu, 1)

            def lower_quarter(dve, i, q):
                dve.wait_ge(s_wu, 4 * i + q + 1)
                dve.tensor_tensor(wq_lo[:, q % 2].bitcast(F32R), quarter(i, q), wq_hi[:, q % 2], ALU.subtract).then_inc(s_wl, 1)

            lbt = zl[:, 0:2, :, :]
            bank = [4 * (i % 2) for i in range(8)]
            s_act, s_dve = sem("proj_copied_act"), sem("proj_copied_dve")
            s_lb, s_lb0, s_lbe = sem("bounds_loaded"), sem("bounds_less_max"), sem("bounds_exp")
            mx = zc[:, 0, :, :]
            by_dve = [g in (1, 2, 5, 7) for g in GROUP_ORDER]
            with nc.Block() as block:
                @block.sync
                def _(sp):
                    load_until(sp, loadable(WIN + 8))

                @block.tensor
                def _(pe):
                    for i, g in enumerate(GROUP_ORDER):
                        if i >= 2:
                            pe.wait_ge(s_act, i - 1)
                            if any(by_dve[:i - 1]):
                                pe.wait_ge(s_dve, sum(by_dve[:i - 1]))
                        for q in range(4):
                            if i == 0:
                                pe.wait_ge(s_xl, 2 if q < 2 else 4)
                            pe.wait_ge(s_wl, 4 * i + q + 1)
                            for xu, xl, b in ((hTu, hTl, 0), (hcTu, hcTl, 2))[:2 if g in WITH_CTX else 1]:
                                for k in range(2 * q, 2 * q + 2):
                                    for t in range(TT):
                                        cols = slice(P * t, P * (t + 1))
                                        mm = product(pe, ps[:, bank[i] + b + t, :], (xu[:, k, cols].bitcast(F32R), xl[:, k, cols].bitcast(F32R)),
                                                     (wq_hi[:, q % 2, k % 2, :].bitcast(F32R), wq_lo[:, q % 2, k % 2, :].bitcast(F32R)),
                                                     k == 0, k == KT - 1)
                            mm.then_inc(ring_used if q == 3 else s_piece, 1)

                @block.scalar
                def _(act):
                    act.dma_start(lbt[:, :, :, :], a["hg_lower_bound"].rearrange("a d n -> (a d n)").partition_broadcast(P)
                                  .rearrange("p (a d n) -> p a d n", a=2, d=2)).then_inc(s_lb, 16)
                    upper_quarter(act, 0, 0)
                    for h in range(2):
                        for x, u in ((hT, hTu), (hcT, hcTu)):
                            act.copy(u[:, 4 * h:4 * h + 4, :].bitcast(F32R), x[:, 4 * h:4 * h + 4, :]).then_inc(s_xu, 1)
                    upper_quarter(act, 0, 1)
                    act.wait_ge(s_lb0, 1)
                    act.activation(lbt[:, :, :, :], lbt[:, :, :, :], ACT.Exp).then_inc(s_lbe, 1)
                    upper_quarter(act, 0, 2)
                    upper_quarter(act, 0, 3)
                    for i, g in enumerate(GROUP_ORDER):
                        if i < 7:
                            upper_quarter(act, i + 1, 0)
                        act.wait_ge(ring_used, WIN + i + 1)
                        if i < 7:
                            upper_quarter(act, i + 1, 1)
                        if g == 1:
                            act.wait_ge(s_dve, 1)
                        lat, ctx_ = ps[:, bank[i]:bank[i] + 2, :], ps[:, bank[i] + 2:bank[i] + 4, :]
                        if g in (3, 4):
                            act.activation(zl[:, g, :, :], lat, ACT.Sigmoid)
                            act.activation(zc[:, g - 1, :, :], ctx_, ACT.Sigmoid).then_inc(s_act, 1)
                        else:
                            act.activation(zl[:, g, :, :], lat, ACT.Sigmoid if g == 7 else ACT.Identity).then_inc(s_act, 1)
                        if i < 7:
                            upper_quarter(act, i + 1, 2)
                            upper_quarter(act, i + 1, 3)

                @block.vector
                def _(dve):
                    lower_quarter(dve, 0, 0)
                    n = 0
                    for h in range(2):
                        for x, u, l in ((hT, hTu, hTl), (hcT, hcTu, hcTl)):
                            n += 1
                            dve.wait_ge(s_xu, n)
                            ks = slice(4 * h, 4 * h + 4)
                            dve.tensor_tensor(l[:, ks, :].bitcast(F32R), x[:, ks, :], u[:, ks, :], ALU.subtract).then_inc(s_xl, 1)
                    lower_quarter(dve, 0, 1)
                    dve.wait_ge(s_lb, 16)
                    dve_link.link(dve, dve.tensor_tensor(mx, lbt[:, 0], lbt[:, 1], ALU.max))
                    for r in range(2):
                        last = dve.tensor_tensor(lbt[:, r], lbt[:, r], mx, ALU.subtract)
                    last.then_inc(s_lb0, 1)
                    lower_quarter(dve, 0, 2)
                    lower_quarter(dve, 0, 3)
                    dve.wait_ge(s_lbe, 1)
                    dve_link.link(dve, dve.tensor_tensor(mx, lbt[:, 0], lbt[:, 1], ALU.add))
                    dve_link.link(dve, dve.reciprocal(mx, mx))
                    dve_link.link(dve, dve.tensor_tensor(lbt[:, 0], lbt[:, 0], mx, ALU.mult))
                    dve_link.link(dve, dve.tensor_scalar(lbt[:, 1], lbt[:, 0], -1.0, 1.0, ALU.mult, ALU.add))
                    for i, g in enumerate(GROUP_ORDER):
                        if i < 7:
                            lower_quarter(dve, i + 1, 0)
                            lower_quarter(dve, i + 1, 1)
                        if g in (1, 2, 5):
                            dve.wait_ge(ring_used, WIN + i + 1)
                            dve.tensor_copy(zc[:, g - 1, :, :], ps[:, bank[i] + 2:bank[i] + 4, :]).then_inc(s_dve, 1)
                        if g in (3, 4, 7):
                            dve.wait_ge(s_act, i + 1)
                        if g == 7:
                            dve.tensor_tensor(zl[:, 7, :, :], zl[:, 7, :, :], ps[:, bank[i]:bank[i] + 2, :], ALU.mult).then_inc(s_dve, 1)
                        if i < 7:
                            lower_quarter(dve, i + 1, 2)
                            lower_quarter(dve, i + 1, 3)
                        if g == 0:
                            dve.wait_ge(s_act, i + 1)
                            for x in (zl[:, 0, :, :], zl[:, 1, :, :]):
                                for t in range(TT):
                                    dve_link.link(dve, rotate(dve, dve_link, x[:, t, :], t))
                        if g in (3, 4):
                            for z in (zl[:, g, :, :], zc[:, g - 1, :, :]):
                                for row, op in ((lbt[:, 1, g - 3, :], ALU.mult), (lbt[:, 0, g - 3, :], ALU.add)):
                                    dve_link.link(dve, dve.tensor_tensor(z, z, row.unsqueeze(1).to_broadcast([P, TT, GW]), op))

    def attend_stage():
        st = ExitStack()
        with st:
            rq, rk = zl[:, 0, :, :], zl[:, 1, :, :]
            qT, kT = hT[:, 0:4, :], hcT[:, :, :].rearrange("p (h a) t -> p h (a t)", a=2)
            ab = hT[:, 4:6, :].rearrange("p a t -> p (a t)")
            aT = hT[:, 6:8, :].rearrange("p a (b q) -> p (a b) q", q=P)
            pe_ = sb("p_exp", [P, 2, 2, 2 * T], stack=st)
            st8 = sb("attn_stats", [P, 8, 8], stack=st)
            lam = small[:, 16:24]
            s_t, s_tc, s_s, s_max, s_p, s_a, s_aT, s_aTc, s_o, s_oc = (sem(n) for n in (
                "qk_turned", "qk_copied", "scores", "score_max", "probs", "prob_diff", "diff_turned", "diffT_copied",
                "attn_out", "attn_out_copied"))
            s_le, s_lam = sem("lambda_exp"), sem("lambda_ready")
            units = [(h, t) for h in range(HEADS) for t in range(TT)]

            def head_out(dve, n):
                h, t = units[n]
                dve.wait_ge(s_o, n + 1)
                dve.tensor_copy(mix[:, t, P * h:P * (h + 1)], ps[:, 6 + n % 2, 0:P]).then_inc(s_oc, 1)

            with nc.Block() as block:
                @block.sync
                def _(sp):
                    load_until(sp, loadable(WIN + 8))

                @block.vector
                def _(dve):
                    for i in range(2):
                        dve_link.link(dve, dve.tensor_tensor_reduce(lams[:, 2 * i, :], lams[:, 2 * i, :], lams[:, 2 * i + 1, :], 1.0, 0.0,
                                                                    ALU.mult, ALU.add, lam[:, i:i + 1]))
                    dve.engine_nop().then_inc(s_le, 1)
                    dve.wait_ge(s_lam, 1)
                    dve_link.link(dve, dve.scalar_tensor_tensor(lam[:, 4:5], lam[:, 2:3], LAMBDA_INIT, lam[:, 3:4], ALU.add, ALU.subtract))
                    for g in range(HEADS):
                        dve.wait_ge(s_t, 2 * g + 2)
                        dve.tensor_copy(qT[:, g, :], ps[:, 2 * (g % 2) + 1, 0:T]).then_inc(s_tc, 1)
                    for n, (h, t) in enumerate(units):
                        x = st8[:, n, :]
                        b = 2 * (n % 2)
                        dve.wait_ge(s_s, n + 1)
                        dve_link.link(dve, dve.tensor_reduce(x[:, 0:2], ps[:, b:b + 2, :], AX, ALU.max))
                        dve.tensor_scalar(x[:, 0:2], x[:, 0:2], -DH ** -0.5, None, ALU.mult).then_inc(s_max, 1)
                        dve.wait_ge(s_p, n + 1)
                        dve_link.link(dve, dve.reciprocal(x[:, 4:6], x[:, 2:4]))
                        dve_link.link(dve, dve.scalar_tensor_tensor(x[:, 6:7], x[:, 5:6], -1.0, lam[:, 4:5], ALU.mult, ALU.mult))
                        if n >= 1:
                            dve.wait_ge(s_aT, n)
                        dve_link.link(dve, dve.tensor_scalar(ab[:, :], pe_[:, n % 2, 0, :], x[:, 4:5], None, ALU.mult))
                        dve.scalar_tensor_tensor(ab[:, :], pe_[:, n % 2, 1, :], x[:, 6:7], ab[:, :], ALU.mult, ALU.add).then_inc(s_a, 1)
                        if n >= 1:
                            head_out(dve, n - 1)
                    head_out(dve, len(units) - 1)
                    dve.wait_ge(s_oc, len(units))

                @block.scalar
                def _(act):
                    act.wait_ge(s_le, 1)
                    act.activation(lam[:, 2:4], lam[:, 0:2], ACT.Exp).then_inc(s_lam, 1)
                    for g in range(HEADS):
                        act.wait_ge(s_t, 2 * g + 1)
                        act.copy(kT[:, g, :], ps[:, 2 * (g % 2), :]).then_inc(s_tk, 1)
                    for n, (h, t) in enumerate(units):
                        x = st8[:, n, :]
                        act.wait_ge(s_max, n + 1)
                        if n >= 2:
                            act.wait_ge(s_a, n - 1)
                        for i in range(2):
                            last = act.activation(pe_[:, n % 2, i, :], ps[:, 2 * (n % 2) + i, :], ACT.Exp, scale=DH ** -0.5,
                                                  bias=x[:, i:i + 1], accum_out=x[:, 2 + i:3 + i])
                        last.then_inc(s_p, 1)
                        act.wait_ge(s_aT, n + 1)
                        if n >= 1:
                            act.wait_ge(s_o, n)
                        act.copy(aT[:, :, :], ps[:, 4 + n % 2, :].rearrange("p (k q) -> p k q", k=4)).then_inc(s_aTc, 1)

                @block.tensor
                def _(pe):
                    for g in range(HEADS):
                        if g >= 2:
                            pe.wait_ge(s_tk, g - 1)
                            pe.wait_ge(s_tc, g - 1)
                        cols = slice(P * g, P * (g + 1))
                        for t in range(TT):
                            pe.transpose(ps[:, 2 * (g % 2), P * t:P * (t + 1)], zc[:, 0, t, cols], ident)
                        for t in range(TT):
                            mm = pe.transpose(ps[:, 2 * (g % 2), T + P * t:T + P * (t + 1)], rk[:, t, cols], ident)
                        mm.then_inc(s_t, 1)
                        for t in range(TT):
                            mm = pe.transpose(ps[:, 2 * (g % 2) + 1, P * t:P * (t + 1)], rq[:, t, cols], ident)
                        mm.then_inc(s_t, 1)
                    pe.wait_ge(s_tk, HEADS)
                    pe.wait_ge(s_tc, HEADS)

                    def scores(n):
                        h, t = units[n]
                        if n >= 2:
                            pe.wait_ge(s_p, n - 1)
                        for i in range(2):
                            mm = pe.matmul(ps[:, 2 * (n % 2) + i, :], qT[DH * i:DH * (i + 1), h, P * t:P * (t + 1)],
                                           kT[DH * i:DH * (i + 1), h, :], start=True, stop=True)
                        mm.then_inc(s_s, 1)

                    scores(0)
                    for n, (h, t) in enumerate(units):
                        if n + 1 < len(units):
                            scores(n + 1)
                        pe.wait_ge(s_a, n + 1)
                        if n >= 2:
                            pe.wait_ge(s_aTc, n - 1)
                        for k in range(4):
                            mm = pe.transpose(ps[:, 4 + n % 2, P * k:P * (k + 1)], ab[:, P * k:P * (k + 1)], ident)
                        mm.then_inc(s_aT, 1)
                        pe.wait_ge(s_aTc, n + 1)
                        if n >= 2:
                            pe.wait_ge(s_oc, n - 1)
                        for k in range(4):
                            v = zc[:, 1, k, P * h:P * (h + 1)] if k < TT else zl[:, 2, k - TT, P * h:P * (h + 1)]
                            mm = pe.matmul(ps[:, 6 + n % 2, 0:P], aT[:, k, :], v, start=(k == 0), stop=(k == 3))
                        mm.then_inc(s_o, 1)

    s_tk = sem("k_copied")
    project_stage()
    slots[3] = mb("ring_3", [P, CHUNK])[:, :]
    attend_stage()
    def recurrence_stage():
        st = ExitStack()
        with st:
            QT = hT[:, 0:4, :].rearrange("p (t a) (b r) -> p t (a b) r", t=TT, r=P)
            KK = hT[:, 4:8, :].rearrange("p (t a) (b r) -> p t (a b) r", t=TT, r=P)
            kz = sb("k_gate", [P, 2, 2, TT, GW], stack=st)
            mov = sb("decay_mov", [P, 2, 9, P], stack=st)
            mask = sb("level_mask", [P, 2, len(LEVELS), P // 4], I32, stack=st)
            S0 = sb("state", [P, HEADS, P], stack=st)
            X = zl[:, 0:2, :, :].rearrange("p b t (h r) -> p b t h r", h=HEADS)
            A = zl[:, 2, :, :].rearrange("p t (h r) -> p t h r", h=HEADS)
            KT = zc[:, 0, :, :].rearrange("p t (h r) -> p t h r", h=HEADS)
            o = zc[:, 1, :, :]
            s_tab = sem("decay_tables_loaded")
            s_f = sem("k_ready")
            lf = [[zl[:, 3 + d, :, :], zc[:, 2 + d, :, :]] for d in range(2)]

            def heads(x):
                return x.rearrange("p t (h v) -> p t h v", v=P)

            def modulation_part(pe, k0, b0):
                for k in range(k0, k0 + 4):
                    w = chunk(pe, ADA2 + k, 1)
                    for j in range(8):
                        mm = pe.matmul(ps[32 * (j % 4):32 * (j % 4) + 32, b0 + j // 4, :], silu_c[:, k, :], w[:, 0, GW * j:GW * (j + 1)],
                                       start=(k == k0), stop=(k == k0 + 3), skip_group_check=True)
                    mm.then_inc(ring_used, 1)

            with nc.Block() as block:
                @block.tensor
                def _(pe):
                    modulation_part(pe, 0, 0)

                @block.sync
                def _(sp):
                    sp.dma_start(mov[:, :, :, :].rearrange("p d n t -> p (d n t)"), a["decay_ops"]).then_inc(s_tab, 16)
                    sp.dma_start(mask[:, :, :, :].rearrange("p d n t -> p (d n t)"), a["level_masks"]).then_inc(s_tab, 16)
                    load_until(sp, loadable(ADA2 + 4))

                @block.scalar
                def _(act):
                    for c in range(2):
                        for d in range(2):
                            act.wait_ge(s_f, 2 * c + d + 1)
                            act.activation(lf[d][c], lf[d][c], ACT.Ln)

                @block.vector
                def _(dve):
                    for c in range(2):
                        for d in range(2):
                            dve.tensor_scalar(kz[:, d, c, :, :], lf[d][c], -1.0, 1.0, ALU.mult, ALU.add).then_inc(s_f, 1)
                    tmp = X[:, 0, :, :, :].rearrange("p t h r -> p t (h r)")
                    for t in range(TT):
                        o = mix[:, t, 0:GW].rearrange("p (h v) -> p h v", v=P)
                        dve_link.link(dve, dve.tensor_tensor(tmp[:, t, :], mix[:, t, 0:GW], mix[:, t, 0:GW], ALU.mult))
                        dve_link.link(dve, dve.tensor_reduce(small[:, 32 + 4 * t:36 + 4 * t], tmp[:, t, :].rearrange("p (h v) -> p h v", v=P), AX, ALU.add))
                    inverse_rms(dve, dve_link, small[:, 32:40], small[:, 40:48], small[:, 48:56], P, EPS)
                    for t in range(TT):
                        for h in range(HEADS):
                            dve_link.link(dve, dve.scalar_tensor_tensor(mix[:, t, P * h:P * (h + 1)], mix[:, t, P * h:P * (h + 1)],
                                                                        small[:, 48 + 4 * t + h:49 + 4 * t + h], subln[:, 0, :], ALU.mult, ALU.mult))
                    dve_link.link(dve, dve.tensor_scalar(mix[:, :, 0:GW], mix[:, :, 0:GW], 1.0 - LAMBDA_INIT, None, ALU.mult))
                    dve.wait_ge(ring_used, ADA2 + 4)
                    dve.tensor_copy(mod_row2[:, :, :], ps[:, 0:2, :])

            s_kk, s_t0, s_t1 = sem("k_sum"), sem("qk_turn"), sem("qk_turned_copied")
            with nc.Block() as block:
                @block.sync
                def _(sp):
                    sp.wait_ge(s_tab, 32)

                @block.gpsimd
                def _(pool):
                    pool.tensor_tensor(o[:, :, :], kz[:, 0, 0, :, :], kz[:, 1, 0, :, :], ALU.add).then_inc(s_kk, 1)

                @block.tensor
                def _(pe):
                    pe.wait_ge(s_kk, 1)
                    for n, src in enumerate((zl[:, 6, :, :], o[:, :, :])):
                        for t in range(TT):
                            for h in range(HEADS):
                                mm = pe.transpose(ps[:, 2 * n + t, P * h:P * (h + 1)], heads(src)[:, t, h, :], ident)
                            mm.then_inc(s_t0, 1)
                    pe.wait_ge(s_t1, 4)
                    for t in range(TT):
                        for h in range(HEADS):
                            mm = pe.matmul(ps[:, 4 + t, P * h:P * (h + 1)], KK[:, t, h, :], QT[:, t, h, :], start=True, stop=True)
                        mm.then_inc(s_t0, 1)

                @block.vector
                def _(dve):
                    for n, dst in enumerate((QT, KK)):
                        for t in range(TT):
                            dve.wait_ge(s_t0, 2 * n + t + 1)
                            dve.tensor_copy(dst[:, t, :, :], ps[:, 2 * n + t, :].rearrange("p (h r) -> p h r", h=HEADS)).then_inc(s_t1, 1)

                @block.scalar
                def _(act):
                    for t in range(TT):
                        act.wait_ge(s_t0, 5 + t)
                        last = act.copy(A[:, t, :, :], ps[:, 4 + t, :].rearrange("p (h r) -> p h r", h=HEADS))

            s_D, s_E, s_X, s_S, s_V = (sem(n) for n in ("decay_sums", "decays", "decayed_ready", "level_scores", "scores_merged"))
            s_kt, s_ktc, s_sx, s_kc, s_st, s_stc, s_ax, s_axc, s_oo = (sem(n) for n in (
                "k_turned", "kT_ready", "ctx_decay", "ctx_k_ready", "state_done", "state_copied", "cross_scores",
                "cross_copied", "o_done"))
            s_eo = sem("ctx_exp")
            nl = len(LEVELS)
            for d in range(2):
                first, second = (0, 1) if d == 0 else (1, 0)
                kd, kc = heads(kz[:, d, 0, :, :]), kz[:, d, 1, :, :]
                vc = heads(zc[:, 4, :, :])
                vl = heads(zl[:, 5, :, :])
                with nc.Block() as block:
                    @block.sync
                    def _(sp):
                        if d == 1:
                            load_until(sp, loadable(WOUT))

                    @block.tensor
                    def _(pe):
                        for t in range(TT):
                            for h in range(HEADS):
                                mm = pe.transpose(ps[:, t, P * h:P * (h + 1)], kd[:, t, h, :], ident)
                            mm.then_inc(s_kt, 1)
                        pe.matmul(ps[:, 2 + second, :], mov[:, d, SUF, :], lf[d][1][:, second, :], start=True, stop=True)
                        pe.matmul(ps[:, 2 + first, :], mov[:, d, SUF, :], lf[d][1][:, first, :], start=True, stop=False)
                        pe.matmul(ps[:, 2 + first, :], ones[:, :], lf[d][1][:, second, :], start=False, stop=True).then_inc(s_sx, 1)
                        pe.wait_ge(s_kc, d + 1)
                        for h in range(HEADS):
                            for t in range(TT):
                                mm = pe.matmul(ps[:, 4, P * h:P * (h + 1)], heads(kc)[:, t, h, :], vc[:, t, h, :],
                                               start=(t == 0), stop=(t == TT - 1))
                        mm.then_inc(s_st, 1)
                        if d == 1:
                            modulation_part(pe, 4, 6)

                    @block.vector
                    def _(dve):
                        for t in range(TT):
                            dve.wait_ge(s_kt, 2 * d + t + 1)
                            dve.tensor_copy(KT[:, t, :, :], ps[:, t, :].rearrange("p (h r) -> p h r", h=HEADS)).then_inc(s_ktc, 1)
                        dve.wait_ge(s_eo, d + 1)
                        dve.tensor_tensor(kc, kc, X[:, 0, :, :, :].rearrange("p t h r -> p t (h r)"), ALU.mult).then_inc(s_kc, 1)
                        dve.wait_ge(s_st, 2 * d + 1)
                        dve.tensor_copy(S0[:, :, :], ps[:, 4, :].rearrange("p (h r) -> p h r", h=HEADS)).then_inc(s_stc, 1)
                        if d == 1:
                            dve.wait_ge(ring_used, WOUT)
                            dve.tensor_tensor(mod_row2[:, :, :], mod_row2[:, :, :], ps[:, 6:8, :], ALU.add)

                    @block.scalar
                    def _(act):
                        act.wait_ge(s_sx, 2 * d + 1)
                        act.activation(X[:, 0, :, :, :].rearrange("p t h r -> p t (h r)"), ps[:, 2:4, :], ACT.Exp).then_inc(s_eo, 1)

                with nc.Block() as block:
                    base = d * nl

                    @block.tensor
                    def _(pe):
                        def decay(n):
                            if n >= 2:
                                pe.wait_ge(s_E, base + n - 1)
                            for t in range(TT):
                                for h in range(HEADS):
                                    mm = pe.matmul(ps[:, 2 * (n % 2) + t, P * h:P * (h + 1)], heads(lf[d][0])[:, t, h, :],
                                                   mov[:, d, n, :], start=True, stop=True)
                            mm.then_inc(s_D, 1)

                        decay(0)
                        for n in range(nl):
                            if n + 1 < nl:
                                decay(n + 1)
                            pe.wait_ge(s_X, base + n + 1)
                            if n >= 2:
                                pe.wait_ge(s_V, base + n - 1)
                            for t in range(TT):
                                for h in range(HEADS):
                                    mm = pe.matmul(ps[:, 4 + 2 * (n % 2) + t, P * h:P * (h + 1)], X[:, n % 2, t, h, :], X[:, n % 2, t, h, :],
                                                   start=True, stop=True)
                            mm.then_inc(s_S, 1)

                    @block.scalar
                    def _(act):
                        for n in range(nl):
                            act.wait_ge(s_D, base + n + 1)
                            if n >= 2:
                                act.wait_ge(s_S, base + n - 1)
                            act.activation(X[:, n % 2, :, :, :].rearrange("p t h r -> p t (h r)"), ps[:, 2 * (n % 2):2 * (n % 2) + 2, :],
                                           ACT.Exp).then_inc(s_E, 1)

                    @block.vector
                    def _(dve):
                        def merge(n):
                            dve.wait_ge(s_S, base + n + 1)
                            if base + n:
                                dve.wait_ge(s_V, base + n)
                            for t in range(TT):
                                last = dve.copy_predicated(A[:, t, :, :], mask[:, d, n, :].bitcast(U8).unsqueeze(1).to_broadcast([P, HEADS, P]),
                                                           ps[:, 4 + 2 * (n % 2) + t, :].rearrange("p (h r) -> p h r", h=HEADS))
                            last.then_inc(s_V, 1)

                        for n, m in enumerate(LEVELS):
                            dve.wait_ge(s_E, base + n + 1)
                            for b in range(2):
                                src = QT if (b == 1) == (d == 0) else KT
                                x = X[:, n % 2, :, :, :].rearrange("p t h (n b m) -> p (t h) n b m", b=2, m=m)[:, :, :, b, :]
                                y = src[:, :, :, :].rearrange("p t h (n b m) -> p t h n b m", b=2, m=m)[:, :, :, :, b, :]
                                for t in range(TT):
                                    xx = x[:, HEADS * t:HEADS * (t + 1)].rearrange("p h n m -> p (h n) m")
                                    last = dve.tensor_tensor(xx, xx, y[:, t].rearrange("p h n m -> p (h n) m"), ALU.mult)
                            last.then_inc(s_X, 1)
                            if n >= 1:
                                merge(n - 1)
                        merge(nl - 1)

                with nc.Block() as block:
                    @block.tensor
                    def _(pe):
                        for n, (t, op) in enumerate(((first, PRE), (first, SUF), (second, PRE), (second, PRE))):
                            for h in range(HEADS):
                                mm = pe.matmul(ps[:, n, P * h:P * (h + 1)], heads(lf[d][0])[:, t, h, :], mov[:, d, op, :],
                                               start=True, stop=(n < 3))
                                if n == 3:
                                    mm = pe.matmul(ps[:, n, P * h:P * (h + 1)], heads(lf[d][0])[:, first, h, :], ones[:, :],
                                                   start=False, stop=True)
                        mm.then_inc(s_sx, 1)
                        pe.wait_ge(s_ax, d + 1)
                        for h in range(HEADS):
                            mm = pe.matmul(ps[:, 4, P * h:P * (h + 1)], X[:, 0, 1, h, :], X[:, 1, 0, h, :], start=True, stop=True)
                        mm.then_inc(s_st, 1)
                        pe.wait_ge(s_axc, d + 1)
                        for t in range(TT):
                            q = X[:, 0, 0, :, :] if t == first else X[:, 1, 1, :, :]
                            for h in range(HEADS):
                                terms = [(q[:, h, :], S0[:, h, :])]
                                if t == second:
                                    terms.append((KT[:, 0, h, :], vl[:, first, h, :]))
                                if d == 1:
                                    terms.append((A[:, t, h, :], vl[:, t, h, :]))
                                for i, (l, r) in enumerate(terms):
                                    mm = pe.matmul(ps[:, 6 + t, P * h:P * (h + 1)], l, r, start=(i == 0), stop=(i == len(terms) - 1))
                            mm.then_inc(s_oo, 1)

                    @block.scalar
                    def _(act):
                        act.wait_ge(s_sx, 2 * d + 2)
                        act.activation(X[:, :, :, :, :].rearrange("p b t h r -> p (b t) (h r)"), ps[:, 0:4, :], ACT.Exp).then_inc(s_eo2, 1)
                        act.wait_ge(s_st, 2 * d + 2)
                        act.copy(KT[:, 0, :, :], ps[:, 4, :].rearrange("p (h r) -> p h r", h=HEADS)).then_inc(s_axc, 1)

                    @block.vector
                    def _(dve):
                        dve.wait_ge(s_eo2, d + 1)
                        for n, (t, src) in enumerate(((first, QT), (first, KT), (second, QT), (second, QT))):
                            xx = X[:, n // 2, n % 2, :, :]
                            last = dve.tensor_tensor(xx, xx, src[:, t, :, :], ALU.mult)
                        last.then_inc(s_ax, 1)
                        for t in range(TT):
                            dve.wait_ge(s_oo, 2 * d + t + 1)
                            if d == 0:
                                last = dve.tensor_copy(o[:, t, :], ps[:, 6 + t, :])
                            else:
                                last = dve.tensor_tensor(o[:, t, :], o[:, t, :], ps[:, 6 + t, :], ALU.add)
                        dve_link.link(dve, last)

    s_eo2 = sem("far_exp")
    recurrence_stage()
    class Turns:

        def __init__(self):
            self.turned, self.even, self.odd = sem("tile_turned"), sem("even_tile_out"), sem("odd_tile_out")
            self.n = self.ne = self.no = 0

        def use(self, n):
            now = (self.n, self.ne, self.no, n)
            self.n, self.ne, self.no = self.n + n, self.ne + (n + 1) // 2, self.no + n // 2
            return now

        def pe(self, pe, now, src, b0):
            n0, e0, o0, n = now
            for k in range(n):
                if k >= 4:
                    pe.wait_ge(self.odd if k % 2 else self.even, (o0 if k % 2 else e0) + k // 2 - 1)
                for t in range(TT):
                    mm = pe.transpose(ps[:, b0 + k % 4, P * t:P * (t + 1)], src[:, t, P * k:P * (k + 1)], ident)
                mm.then_inc(self.turned, 1)

        def dve(self, dve, now, dst, b0, scale=None, bias=None):
            n0, e0, o0, n = now
            for k in range(0, n, 2):
                dve.wait_ge(self.turned, n0 + k + 1)
                x = ps[:, b0 + k % 4, 0:T]
                if scale is None:
                    ins = dve.tensor_copy(dst[:, k, :], x)
                elif bias is None:
                    ins = dve.tensor_scalar(dst[:, k, :], x, scale[:, k:k + 1], None, ALU.mult)
                else:
                    ins = dve.tensor_scalar(dst[:, k, :], x, scale[:, k:k + 1], bias[:, k:k + 1], ALU.mult, ALU.add)
                ins.then_inc(self.even, 1)

        def act(self, act, now, dst, b0, scale=None, bias=None):
            n0, e0, o0, n = now
            for k in range(1, n, 2):
                act.wait_ge(self.turned, n0 + k + 1)
                x = ps[:, b0 + k % 4, 0:T]
                if scale is None:
                    ins = act.copy(dst[:, k, :], x)
                elif bias is None:
                    ins = act.activation(dst[:, k, :], x, ACT.Identity, scale=scale[:, k:k + 1])
                else:
                    ins = act.activation(dst[:, k, :], x, ACT.Identity, scale=scale[:, k:k + 1], bias=bias[:, k:k + 1])
                ins.then_inc(self.odd, 1)

        def wait_all(self, eng, now):
            n0, e0, o0, n = now
            eng.wait_ge(self.even, e0 + (n + 1) // 2)
            if n > 1:
                eng.wait_ge(self.odd, o0 + n // 2)

    turns = Turns()
    s_sq = Tally(sem("squares_summed"))

    def square_sums(act, tiles, junk, ss):
        for j, x in enumerate(tiles):
            act.activation(junk, x, ACT.Square, accum_out=ss[:, j:j + 1]).then_inc(s_sq.sem, 1)
            s_sq.n += 1
            act.wait_ge(s_sq.sem, s_sq.n)

    def out_stage():
        st = ExitStack()
        with st:
            bg = sb("b_gates", [P, 2, D], stack=st)
            tmp = sb("out_tmp", [P, TT, D], stack=st)
            modT = sb("modT2", [P, 2, KT], stack=st)
            ss, v, rstd = small[:, 0:2], small[:, 2:4], small[:, 4:6]
            s_bg, s_g, s_gc, s_mt = (sem(n) for n in (
                "gate_bias_loaded", "gate_rows", "gate_rows_out", "mod2_turned"))
            first, second = turns.use(4), turns.use(4)
            s_hg = sem("recurrence_normed")
            o, sq_tmp = zc[:, 1, :, :], zl[:, 0, :, :]
            sq = s_sq.n
            with nc.Block() as block:
                @block.sync
                def _(sp):
                    sp.dma_start(bg[:, 0, :], a["b_ada"][0, 2 * D:3 * D].partition_broadcast(P)).then_inc(s_bg, 16)
                    sp.dma_start(bg[:, 1, :], a["b_ada"][0, 5 * D:6 * D].partition_broadcast(P)).then_inc(s_bg, 16)
                    load_until(sp, loadable(MOE))

                @block.tensor
                def _(pe):
                    turns.pe(pe, first, mix[:, :, 0:GW], 4)
                    turns.wait_all(pe, first)
                    def out_product(i):
                        w = chunk(pe, WOUT + i, 4)
                        for kk in range(4):
                            k = 4 * i + kk
                            for t in range(TT):
                                for b in range(2):
                                    mm = pe.matmul(ps[:, 4 + 2 * t + b, :], hT[:, k, P * t:P * (t + 1)], w[:, kk, GW * b:GW * (b + 1)],
                                                   start=(k == 0), stop=(k == KT - 1))
                        mm.then_inc(ring_used, 1)

                    def gate_rows(r):
                        for b in range(2):
                            j = 2 * r + b
                            mm = pe.matmul(ps[:, 2 + b, :], cst[:, C_SEL + P * j:C_SEL + P * (j + 1)], mod_row2[:, r, :], start=True, stop=True)
                        mm.then_inc(s_g, 1)

                    gate_rows(0)
                    out_product(0)
                    pe.wait_ge(s_gc, 1)
                    pe.wait_ge(s_hg, 1)
                    turns.pe(pe, second, mix[:, :, GW:D], 0)
                    turns.wait_all(pe, second)
                    gate_rows(1)
                    for r in range(2):
                        for q in range(4):
                            mm = pe.transpose(ps[:, r, P * q:P * (q + 1)], mod_row2[:, r, P * q:P * (q + 1)], ident)
                    mm.then_inc(s_mt, 1)
                    out_product(1)

                @block.scalar
                def _(act):
                    turns.act(act, first, hT[:, 0:4, :], 4)
                    turns.act(act, second, hT[:, 4:8, :], 0)
                    act.wait_ge(ring_used, MOE)
                    square_sums(act, [ps[:, 4 + 2 * t:6 + 2 * t, :] for t in range(TT)], tmp[:, 0, :].rearrange("p (a b) -> p a b", a=2), ss)

                @block.vector
                def _(dve):
                    turns.dve(dve, first, hT[:, 0:4, :], 4)
                    dve.wait_ge(s_bg, 32)
                    def gate_row(r, row):
                        dve.wait_ge(s_g, r + 1)
                        y = ps[:, 2:4, :].rearrange("p a b -> p (a b)")
                        dve_link.link(dve, dve.tensor_tensor(bg[:, r, :], y, bg[:, r, :], ALU.add))
                        dve.tensor_tensor(row[:, :], row[:, :], bg[:, r, :], ALU.mult).then_inc(s_gc, 1)

                    gate_row(0, g1row)
                    dve_link.link(dve, dve.tensor_tensor(sq_tmp, o, o, ALU.mult))
                    dve_link.link(dve, dve.tensor_reduce(small[:, 32:40], sq_tmp.rearrange("p t (h v) -> p t h v", v=P), AX, ALU.add))
                    inverse_rms(dve, dve_link, small[:, 32:40], small[:, 40:48], small[:, 48:56], P, EPS)
                    for t in range(TT):
                        for h in range(HEADS):
                            last = dve.scalar_tensor_tensor(o[:, t, P * h:P * (h + 1)], o[:, t, P * h:P * (h + 1)],
                                                            small[:, 48 + 4 * t + h:49 + 4 * t + h], subln[:, 1, :], ALU.mult, ALU.mult)
                    dve_link.link(dve, last)
                    dve.tensor_tensor(mix[:, :, GW:D], zl[:, 7, :, :], o, ALU.mult).then_inc(s_hg, 1)
                    turns.dve(dve, second, hT[:, 4:8, :], 0)
                    gate_row(1, g2row)
                    dve.wait_ge(s_mt, 1)
                    for i, (bank, j) in enumerate(((0, 2), (1, 0))):
                        x = ps[:, bank, :].rearrange("p (q j s) -> p j q s", q=4, j=4)[:, j:j + 2, :, 0]
                        last = dve.tensor_copy(modT[:, i, :].rearrange("p (j q) -> p j q", j=2), x)
                    dve_link.link(dve, last)
                    dve.tensor_tensor(affA[:, 0, 1, :], modT[:, 0, :], feat[:, F_ADA + 24:F_ADA + 32], ALU.add)
                    dve_link.link(dve, dve.tensor_tensor(modT[:, 1, :], modT[:, 1, :], feat[:, F_ADA + 32:F_ADA + 40], ALU.add))
                    dve.scalar_tensor_tensor(affA[:, 0, 0, :], modT[:, 1, :], 1.0, feat[:, F_NPF:F_NPF + 8], ALU.add, ALU.mult)
                    dve.wait_ge(s_sq.sem, sq + 2)
                    inverse_rms(dve, dve_link, ss, v, rstd, D, EPS)
                    dve.wait_ge(s_gc, 2)
                    for t in range(TT):
                        dve_link.link(dve, dve.scalar_tensor_tensor(tmp[:, t, :], ps[:, 4 + 2 * t:6 + 2 * t, :].rearrange("p a b -> p (a b)"),
                                                                    rstd[:, t:t + 1], g1row[:, :], ALU.mult, ALU.mult))
                        dve_link.link(dve, dve.tensor_tensor(xres[:, t, :], xres[:, t, :], tmp[:, t, :], ALU.add))

    out_stage()
    mixer_stack.close()
    kmT = sb("mem_kT", [P, 2, 2, T])
    vm = sb("mem_v", [P, 2, TT, 256])
    ring_stack = ctx.enter_context(ExitStack())
    ring_hi = sb("ring_hi", [P, 5, CHUNK], stack=ring_stack)
    slots[3:8] = [ring_hi[:, s, :] for s in range(5)]

    moe_stack = ctx.enter_context(ExitStack())
    xinT = sb("xinT", [P, KT, EXPERTS * CAP], stack=moe_stack)
    buf4 = sb("buf4", [P, D], stack=moe_stack)
    scat = sb("scatter_w", [P, NGROUPS, T], stack=moe_stack)
    xg = sb("x_group", [P, KT, P], stack=moe_stack)
    scat_g = sb("scatter_group", [P, T], stack=moe_stack)

    def norm_sums(act, junk):
        square_sums(act, [xres[:, t, :] for t in range(TT)], junk, small[:, 0:2])

    def norm_scale(dve, at, xn):
        ss, v, rstd = small[:, 0:2], small[:, 2:4], small[:, 4:6]
        dve.wait_ge(s_sq.sem, at)
        inverse_rms(dve, dve_link, ss, v, rstd, D, EPS)
        for t in range(TT):
            last = dve.tensor_scalar(xn[:, t, :], xres[:, t, :], rstd[:, t:t + 1], None, ALU.mult)
        last.then_inc(s_xnr.sem, 1)
        s_xnr.n += 1

    s_xnr = Tally(sem("xn_ready"))

    def router_stage():
        st = ExitStack()
        with st:
            wr = sb("w_router", [P, KT, EXPERTS], stack=st)
            aff = sb("affinity", [P, TT, EXPERTS], stack=st)
            cur, vals = scat_g[0:EXPERTS, :], sb("top_vals", [EXPERTS, CAP], stack=st)
            idx, idxf = sb("top_idx", [EXPERTS, CAP], U32, stack=st), sb("top_idxf", [EXPERTS, CAP], stack=st)
            diag = xg[0:EXPERTS, :, :].rearrange("p k n -> p (k n)").rearrange("p (i e c) -> p i e c", i=2, e=EXPERTS)
            col = sb("slot_cols", [P, 2, NGROUPS], stack=st)
            pick = buf4[:, :].rearrange("p (t s) -> p t s", t=TT)
            stat = small[:, 8:16]
            xn = mix
            s_wr, s_lg, s_sm, s_ex, s_af, s_at, s_dg, s_rc, s_pk, s_g, s_gx, s_gy = (sem(n) for n in (
                "router_loaded", "logits", "logit_max", "aff_exp", "aff_ready", "aff_turned", "diag_ready", "slots_spread", "picks_ready",
                "gathered", "gather_even", "gather_odd"))
            at = s_sq.n + TT
            now = turns.use(KT)
            xr = s_xnr.n + 1
            with nc.Block() as block:
                @block.sync
                def _(sp):
                    sp.dma_start(wr[:, :, :], a["w_router"][0].rearrange("(k p) e -> p k e", p=P)).then_inc(s_wr, 16)
                    load_until(sp, MOE + 8)

                @block.scalar
                def _(act):
                    norm_sums(act, buf4[:, :])
                    turns.act(act, now, hT, 4, affA[:, 0, 0, :], affA[:, 0, 1, :])
                    act.wait_ge(s_sm, 1)
                    act.activation(aff[:, :, :], aff[:, :, :], ACT.Exp).then_inc(s_ex, 1)
                    for k in range(1, KT, 2):
                        act.wait_ge(s_g, k + 1)
                        act.activation(xinT[:, k, :], ps[:, 4 + k % 4, :], ACT.Identity, scale=affA[:, 0, 0, k:k + 1],
                                       bias=affA[:, 0, 1, k:k + 1]).then_inc(s_gy, 1)

                @block.tensor
                def _(pe):
                    pe.wait_ge(s_xnr.sem, xr)
                    turns.pe(pe, now, xn, 4)
                    turns.wait_all(pe, now)
                    pe.wait_ge(s_wr, 16)
                    for t in range(TT):
                        for k in range(KT):
                            mm = pe.matmul(ps[:, 0, EXPERTS * t:EXPERTS * (t + 1)], hT[:, k, P * t:P * (t + 1)], wr[:, k, :],
                                           start=(k == 0), stop=(k == KT - 1))
                    mm.then_inc(s_lg, 1)
                    pe.wait_ge(s_af, 1)
                    for t in range(TT):
                        mm = pe.transpose(ps[0:EXPERTS, 1, P * t:P * (t + 1)], aff[:, t, :], ident)
                    mm.then_inc(s_at, 1)
                    pe.wait_ge(s_dg, 1)
                    pe.matmul(ps[:, 2, :], ones[0:EXPERTS, :], diag[:, 0, :, :].rearrange("p e c -> p (e c)"), start=True, stop=True)
                    for i in range(2):
                        for g in range(NGROUPS):
                            mm = pe.matmul(ps[:, 3, 4 * i + g:4 * i + g + 1], diag[:, i, 4 * g:4 * (g + 1), :].rearrange("p e c -> p (e c)"),
                                           ones[0:EXPERTS, 0:1], start=True, stop=True)
                    mm.then_inc(s_rc, 1)
                    pe.wait_ge(s_pk, 1)
                    for k in range(KT):
                        if k >= 4:
                            pe.wait_ge(s_gy if k % 2 else s_gx, k // 2 - 1)
                        for t in range(TT):
                            mm = pe.matmul(ps[:, 4 + k % 4, :], xn[:, t, P * k:P * (k + 1)], pick[:, t, :], start=(t == 0), stop=(t == TT - 1))
                        mm.then_inc(s_g, 1)

                @block.vector
                def _(dve):
                    norm_scale(dve, at, xn)
                    turns.dve(dve, now, hT, 4, affA[:, 0, 0, :], affA[:, 0, 1, :])
                    dve.wait_ge(s_lg, 1)
                    lg = ps[:, 0, 0:TT * EXPERTS].rearrange("p (t e) -> p t e", t=TT)
                    dve_link.link(dve, dve.tensor_reduce(stat[:, 0:2], lg, AX, ALU.max))
                    dve.tensor_tensor(aff[:, :, :], lg, stat[:, 0:2].unsqueeze(2).to_broadcast([P, TT, EXPERTS]), ALU.subtract).then_inc(s_sm, 1)
                    dve.wait_ge(s_ex, 1)
                    dve_link.link(dve, dve.tensor_reduce(stat[:, 2:4], aff[:, :, :], AX, ALU.add))
                    dve_link.link(dve, dve.reciprocal(stat[:, 4:6], stat[:, 2:4]))
                    dve.tensor_tensor(aff[:, :, :], aff[:, :, :], stat[:, 4:6].unsqueeze(2).to_broadcast([P, TT, EXPERTS]), ALU.mult).then_inc(s_af, 1)
                    dve.wait_ge(s_at, 1)
                    dve_link.link(dve, dve.tensor_copy(cur[:, :], ps[0:EXPERTS, 1, 0:T]))
                    for r in range(0, CAP, 8):
                        dve_link.link(dve, dve.max(vals[:, r:r + 8], cur[:, :]))
                        dve_link.link(dve, dve.max_index(idx[:, r:r + 8], vals[:, r:r + 8], cur[:, :]))
                        if r + 8 < CAP:
                            dve_link.link(dve, dve.match_replace(cur[:, :], vals[:, r:r + 8], cur[:, :], -1.0))
                    dve_link.link(dve, dve.tensor_copy(idxf[:, :], idx[:, :]))
                    eye = cst[0:EXPERTS, C_EYE:C_EYE + EXPERTS * CAP].rearrange("p (e c) -> p e c", c=CAP)
                    dve.tensor_tensor(diag[:, 0, :, :], eye, idxf[:, :].unsqueeze(1).to_broadcast([EXPERTS, EXPERTS, CAP]), ALU.mult)
                    dve.tensor_tensor(diag[:, 1, :, :], eye, vals[:, :].unsqueeze(1).to_broadcast([EXPERTS, EXPERTS, CAP]), ALU.mult).then_inc(s_dg, 1)
                    dve.wait_ge(s_rc, 1)
                    dve_link.link(dve, dve.tensor_copy(col[:, :, :], ps[:, 3, 0:8].rearrange("p (i g) -> p i g", i=2)))
                    for t in range(TT):
                        last = dve.tensor_scalar(pick[:, t, :], ps[:, 2, :], cst[:, C_TOK + t:C_TOK + t + 1], None, ALU.is_equal)
                    last.then_inc(s_pk, 1)
                    for g in range(NGROUPS):
                        dve.tensor_scalar(scat[:, g, :], cst[:, C_IOTA:C_IOTA + T], col[:, 0, g:g + 1], col[:, 1, g:g + 1], ALU.is_equal, ALU.mult)
                    for k in range(0, KT, 2):
                        dve.wait_ge(s_g, k + 1)
                        dve.tensor_scalar(xinT[:, k, :], ps[:, 4 + k % 4, :], affA[:, 0, 0, k:k + 1], affA[:, 0, 1, k:k + 1],
                                          ALU.mult, ALU.add).then_inc(s_gx, 1)

    router_stage()

    def experts_stage():
        acc = hT[:, :, :].rearrange("p (t a) n -> p t (a n)", t=TT)
        act_in = buf4
        aT, y = mix[:, 0, :].rearrange("p (k s) -> p k s", k=KT), mix[:, 1, :]
        s_xg, s_pg, s_e, s_a, s_t, s_tc, s_yc, s_sc, s_acc = (sem(n) for n in (
            "group_x_ready", "group_scatter_ready", "gate_exp_ready", "hidden_ready", "hidden_turned",
            "hiddenT_ready", "y_ready", "scattered", "sum_ready"))
        s_ao = sem("hiddenT_ready_act")
        base = {c: turn[MOE + c] for c in range(8)}

        with nc.Block() as block:
            @block.sync
            def _(sp):
                def load(g, c, read):
                    if c not in (0, 16):
                        sp.wait_ge(ring_used, read + (1 if c in (15, 23) else 0))
                    s = slot_of(MOE + c)
                    sp.dma_start(slots[s].rearrange("p (e n) -> p e n", e=GROUP), moe_chunk(g, c)).then_inc(loaded[s], 16)

                for t in range(TT):
                    sp.dma_start(mem_tile[t], a["mem_2"][0, P * t:P * (t + 1), :]).then_inc(s_mem, 16)
                with sp.Fori(0, NGROUPS - 1) as g:
                    for c in range(8, 24):
                        load(g, c, g * 24 + (MOE + c - 7))
                    for c in range(8):
                        load(g + 1, c, g * 24 + (MOE + 24 + c - 7))
                for c in range(8, 24):
                    load(NGROUPS - 1, c, (NGROUPS - 1) * 24 + (MOE + min(c, 22) - 7))
                issued[0] = BLOCK2
                load_until(sp, BLOCK2 + 3)

            @block.tensor
            def _(pe):
                with pe.Fori(0, NGROUPS) as g:
                    def weights(c):
                        s = slot_of(MOE + c)
                        pe.wait_ge(loaded[s], g * 48 + 16 * (base[c % 8] + c // 8))
                        return slots[s].rearrange("p (e n) -> p e n", e=GROUP)

                    pe.wait_ge(s_xg, g + 1)
                    for c in range(16):
                        w = weights(c)
                        for b in range(2):
                            for e in range(GROUP):
                                mm = pe.matmul(ps[32 * e:32 * (e + 1), 2 * (c % 2) + b, :], xg[:, c // 2, CAP * e:CAP * (e + 1)],
                                               w[:, e, GW * b:GW * (b + 1)], start=(c < 2), stop=(c >= 14), skip_group_check=True)
                        mm.then_inc(ring_used, 1)
                    pe.wait_ge(s_a, g + 1)
                    for k in range(KT):
                        mm = pe.transpose(ps[:, k // 4, P * (k % 4):P * (k % 4 + 1)], act_in[:, P * k:P * (k + 1)], ident)
                        if k % 4 == 3:
                            mm.then_inc(s_t, 1)
                    pe.wait_ge(s_tc, g + 1)
                    pe.wait_ge(s_ao, g + 1)
                    for c in range(16, 24):
                        w = weights(c)
                        for b in range(2):
                            for e in range(GROUP):
                                mm = pe.matmul(ps[32 * e:32 * (e + 1), 2 + b, :], aT[:, c - 16, CAP * e:CAP * (e + 1)],
                                               w[:, e, GW * b:GW * (b + 1)], start=(c == 16), stop=(c == 23), skip_group_check=True)
                        mm.then_inc(ring_used, 1)
                    pe.wait_ge(s_yc, g + 1)
                    pe.wait_ge(s_pg, g + 1)
                    pe.wait_ge(s_acc, g + 1)
                    for t in range(TT):
                        for b in range(2):
                            mm = pe.matmul(ps[:, 4 + 2 * t + b, :], scat_g[:, P * t:P * (t + 1)], y[:, GW * b:GW * (b + 1)], start=True, stop=True)
                    mm.then_inc(s_sc, 1)

            @block.scalar
            def _(act):
                act.wait_ge(s_mem, 16 * TT)
                for t in range(TT):
                    act.activation(y, mem_tile[t], ACT.Square, accum_out=mss[:, t:t + 1]).then_inc(s_msq, 1)
                    act.wait_ge(s_msq, t + 1)
                with act.Fori(0, NGROUPS) as g:
                    act.wait_ge(ring_used, g * 24 + (MOE + 15))
                    e = act.activation(y.rearrange("p (b n) -> p b n", b=2), ps[:, 0:2, :], ACT.Exp, scale=-1.0)
                    e.then_inc(s_e, 1)
                    act.wait_ge(s_t, 2 * g + 2)
                    act.copy(aT[:, 4:8, :], ps[:, 1, :].rearrange("p (k s) -> p k s", k=4)).then_inc(s_ao, 1)
                    act.wait_ge(ring_used, g * 24 + (MOE + 24))
                    act.copy(y.rearrange("p (b n) -> p b n", b=2), ps[:, 2:4, :]).then_inc(s_yc, 1)
                    act.wait_ge(s_sc, g + 1)

            @block.gpsimd
            def _(pool):
                with pool.Fori(0, NGROUPS) as g:
                    pool.wait_ge(s_sg, g + 1)
                    pool.tensor_copy(scat_g[:, :].unsqueeze(1), scat[:, bass.ds(g, 1), :]).then_inc(s_pg, 1)

            @block.vector
            def _(dve):
                dve.memset(acc, 0.0).then_inc(s_acc, 1)
                dve.tensor_copy(xg[:, :, :], xinT[:, :, 0:P]).then_inc(s_xg, 1)
                dve.wait_ge(s_acc, 1)
                dve.wait_ge(s_xg, 1)
                dve.engine_nop().then_inc(s_sg, 1)
                dve.wait_ge(s_msq, TT)
                inverse_rms(dve, dve_link, mss, mv, mrstd, D, EPS)
                for t in range(TT):
                    dve.tensor_scalar(mem_tile[t], mem_tile[t], mrstd[:, t:t + 1], None, ALU.mult)
                with dve.Fori(0, NGROUPS) as g:
                    dve.wait_ge(s_e, g + 1)
                    e = y
                    dve.tensor_scalar(e, e, 1.0, None, ALU.add).then_inc(s_m, 1)
                    dve.wait_ge(s_m, g * 3 + 1)
                    dve.reciprocal(e, e).then_inc(s_m, 1)
                    dve.wait_ge(s_m, g * 3 + 2)
                    flat = ps[:, :, :].rearrange("p a b -> p (a b)")
                    dve.tensor_tensor(e, e, flat[:, 0:D], ALU.mult).then_inc(s_m, 1)
                    dve.wait_ge(s_m, g * 3 + 3)
                    dve.wait_ge(ring_used, g * 24 + (MOE + 16))
                    dve.tensor_tensor(act_in[:, :], e, flat[:, D:2 * D], ALU.mult).then_inc(s_a, 1)
                    dve.tensor_copy(xg[:, :, :].rearrange("p k s -> p k s"), xnext(g)).then_inc(s_xg, 1)
                    dve.wait_ge(s_t, 2 * g + 1)
                    dve.tensor_copy(aT[:, 0:4, :], ps[:, 0, :].rearrange("p (k s) -> p k s", k=4)).then_inc(s_tc, 1)
                    dve.wait_ge(s_sc, g + 1)
                    for t in range(TT):
                        last = dve.tensor_tensor(acc[:, t, :], acc[:, t, :], flat[:, D * (2 + t):D * (3 + t)], ALU.add)
                    last.then_inc(s_acc, 1)
                    dve.engine_nop().then_inc(s_sg, 1)
                    dve.wait_ge(s_acc, g + 2)

    s_m, s_sg, s_mem, s_msq = sem("gate_step"), sem("scatter_group_free"), sem("mem_loaded"), sem("mem_squares")
    mem_tile = [kmT[:, :, :, :].rearrange("p l a n -> p (l a n)"), vm[:, :, :, :].rearrange("p l t n -> p (l t n)")]
    mss, mv, mrstd = small[:, 24:26], small[:, 26:28], small[:, 28:30]

    def xnext(g):
        return xinT[:, :, bass.ds(((g + 1) % NGROUPS) * P, P)]

    experts_stage()
    moe_stack.close()
    ring_stack.close()
    slots[3:8] = [None] * 5

    fin_row = sb("fin_row", [P, D])
    s_fr = sem("final_gain_loaded")
    w_hi, w_lo = sb("weights_upper", [P, CHUNK]), sb("weights_lower", [P, CHUNK])
    hTu, hTl = sb("hT_upper", [P, KT, T]), sb("hT_lower", [P, KT, T])

    s_xu, s_xl = Tally(sem("hT_upper_ready")), Tally(sem("hT_lower_ready"))

    class SplitTurns:

        def __init__(self, gain):
            self.turned0, self.u0, self.l0, self.gain = turns.n, s_xu.n, s_xl.n, gain
            turns.n, s_xu.n, s_xl.n = turns.n + KT, s_xu.n + KT, s_xl.n + KT

        def pe(self, pe, src):
            for k in range(KT):
                if k >= 4:
                    pe.wait_ge(s_xl.sem, self.l0 + k - 3)
                for t in range(TT):
                    mm = pe.transpose(ps[:, 4 + k % 4, P * t:P * (t + 1)], src[:, t, P * k:P * (k + 1)], ident)
                mm.then_inc(turns.turned, 1)
            pe.wait_ge(s_xl.sem, self.l0 + KT)

        def act(self, act):
            for k in range(KT):
                act.wait_ge(turns.turned, self.turned0 + k + 1)
                act.activation(hTu[:, k, :].bitcast(F32R), ps[:, 4 + k % 4, 0:T], ACT.Identity, scale=self.gain[:, k:k + 1]).then_inc(s_xu.sem, 1)

        def dve(self, dve):
            for k in range(KT):
                dve.wait_ge(s_xu.sem, self.u0 + k + 1)
                dve.scalar_tensor_tensor(hTl[:, k, :].bitcast(F32R), ps[:, 4 + k % 4, 0:T], self.gain[:, k:k + 1], hTu[:, k, :],
                                         ALU.mult, ALU.subtract).then_inc(s_xl.sem, 1)

    def xT(k, cols):
        return hTu[:, k, cols].bitcast(F32R), hTl[:, k, cols].bitcast(F32R)

    def projection(pe, name, cols):
        for i, (k0, kn, parts) in enumerate(cols):
            wu, wl, wait = split_chunk(pe, w_hi, w_lo, where[name] + i)
            for h in range(2):
                wait(h)
                for kk in range(kn // 2 * h, kn // 2 * (h + 1)):
                    k = k0 + kk
                    for t in range(TT):
                        for b, c0, n in parts:
                            mm = product(pe, ps[:, b + t, 0:n], xT(k, slice(P * t, P * (t + 1))), (wu[:, kk, c0:c0 + n], wl[:, kk, c0:c0 + n]),
                                         k == 0, k == KT - 1)
                mm.then_inc(ring_used if h else s_half, 1)

    def projection_out(dve, name, cols, dst):
        for i, (k0, kn, parts) in enumerate(cols):
            if k0 + kn < KT:
                continue
            dve.wait_ge(ring_used, where[name] + i + 1)
            for b, c0, n in parts:
                o0 = c0 + (GW * i if k0 == 0 else 0)
                dve.tensor_copy(dst[:, :, o0:o0 + n], ps[:, b:b + 2, 0:n])

    def normed_projection(name, gain, cols, dst):
        at, w0 = s_sq.n + TT, where[name]
        register_split(*range(w0 + 1, w0 + len(cols)))
        xr = s_xnr.n + 1
        turn = SplitTurns(gain)
        rest = [(w0, 1)] + [(n, h) for n in range(w0 + 1, w0 + len(cols)) for h in range(2)]
        with nc.Block() as block:
            @block.sync
            def _(sp):
                load_until(sp, loadable(w0 + len(cols)))

            @block.scalar
            def _(act):
                norm_sums(act, dst[:, 0, 0:D])
                upper(act, w_hi, w0, 1)
                turn.act(act)
                for n, h in rest[1:]:
                    upper(act, w_hi, n, h)

            @block.tensor
            def _(pe):
                pe.wait_ge(s_xnr.sem, xr)
                turn.pe(pe, mix)
                projection(pe, name, cols)

            @block.vector
            def _(dve):
                norm_scale(dve, at, mix)
                turn.dve(dve)
                for n, h in rest:
                    lower(dve, w_hi, w_lo, n, h)
                projection_out(dve, name, cols, dst)

    s_at = {n: Tally(sem("att_" + n)) for n in ("scores", "max", "probs", "probs_normed", "turned", "turned_copied", "out", "out_upper", "out_copied", "bias")}

    def attention_stage(units, sc, pT, st, nxt):
        before = {n: t.n for n, t in s_at.items()}
        N = len(units)
        register_split(nxt)

        AHEAD = 1

        def done(name, ins):
            ins.then_inc(s_at[name].sem, 1)

        def need(eng, name, n):
            eng.wait_ge(s_at[name].sem, before[name] + n + 1)

        with nc.Block() as block:
            @block.tensor
            def _(pe):
                for i in range(-AHEAD, N + 3):
                    if i + AHEAD < N:
                        n = i + AHEAD
                        q, k, bias, scale, sink, vs, ot, oh, t = units[n]
                        if n >= 2:
                            need(pe, "probs" if units[n - 2][2] is None else "max", n - 2)
                        done("scores", pe.matmul(ps[:, n % 2, 0:P * len(vs)], q, k, start=True, stop=True))
                    n = i - 2
                    if 0 <= n < N:
                        vs = units[n][5]
                        need(pe, "probs_normed", n)
                        if n >= 2:
                            need(pe, "turned_copied", n - 2)
                        for j in range(len(vs)):
                            mm = pe.transpose(ps[:, 2 + n % 2, P * j:P * (j + 1)], sc[:, n % 3, P * j:P * (j + 1)], ident)
                        done("turned", mm)
                    n = i - 3
                    if 0 <= n < N:
                        q, k, bias, scale, sink, vs, ot, oh, t = units[n]
                        need(pe, "turned_copied", n)
                        if n >= 4:
                            need(pe, "out_copied", n - 4)
                        for j, v in enumerate(vs):
                            mm = pe.matmul(ps[64 * oh:64 * oh + 64, 4 + n % 4, 0:P], v, pT[:, n % 2, P * j:P * (j + 1)],
                                           start=(j == 0), stop=(j == len(vs) - 1))
                        done("out", mm)

            @block.scalar
            def _(act):
                for i in range(N + 4):
                    if i in (4, 6):
                        upper(act, w_hi, nxt, (i - 4) // 2)
                    if i < N:
                        q, k, bias, scale, sink, vs, ot, oh, t = units[i]
                        x = st[:, i % 4, :]
                        w = P * len(vs)
                        need(act, "max", i)
                        if i >= 3 and bias is None:
                            need(act, "turned", i - 3)
                        if sink is not None:
                            act.activation(x[:, 3:4], sink, ACT.Exp, bias=x[:, 1:2])
                        src, s = (ps[:, i % 2, 0:w], scale) if bias is None else (sc[:, i % 3, 0:w], 1.0)
                        done("probs", act.activation(sc[:, i % 3, 0:w], src, ACT.Exp, scale=s, bias=x[:, 1:2], accum_out=x[:, 2:3]))
                    n = i - 2
                    if 0 <= n < N:
                        w = P * len(units[n][5])
                        need(act, "turned", n)
                        if n >= 2:
                            need(act, "out", n - 2)
                        done("turned_copied", act.copy(pT[:, n % 2, 0:w], ps[:, 2 + n % 2, 0:w]))
                    n = i - 4
                    if 0 <= n < N:
                        q, k, bias, scale, sink, vs, ot, oh, t = units[n]
                        need(act, "out", n)
                        half = slice(64 * oh, 64 * oh + 64)
                        done("out_upper", act.copy(hTu[half, ot, P * t:P * (t + 1)].bitcast(F32R), ps[half, 4 + n % 4, 0:P]))

            @block.vector
            def _(dve):
                for i in range(N + 5):
                    if i in (4, 6):
                        lower(dve, w_hi, w_lo, nxt, (i - 4) // 2)
                    if i < N:
                        q, k, bias, scale, sink, vs, ot, oh, t = units[i]
                        x = st[:, i % 4, :]
                        w = P * len(vs)
                        need(dve, "scores", i)
                        if i >= 3:
                            need(dve, "turned", i - 3)
                        if bias is None:
                            dve_link.link(dve, dve.tensor_reduce(x[:, 0:1], ps[:, i % 2, 0:w], AX, ALU.max))
                        else:
                            if callable(bias):
                                need(dve, "bias", i)
                                bias = bias(None)
                            dve_link.link(dve, dve.tensor_tensor_reduce(sc[:, i % 3, 0:w], ps[:, i % 2, 0:w], bias, scale,
                                                                        -3.0e38 if sink is None else sink, ALU.add, ALU.max, x[:, 0:1]))
                        done("max", dve.tensor_scalar(x[:, 1:2], x[:, 0:1], -scale if bias is None else -1.0, None, ALU.mult))
                    n = i - 1
                    if 0 <= n < N:
                        q, k, bias, scale, sink, vs, ot, oh, t = units[n]
                        x = st[:, n % 4, :]
                        w = P * len(vs)
                        need(dve, "probs", n)
                        if sink is not None:
                            dve_link.link(dve, dve.tensor_tensor(x[:, 2:3], x[:, 2:3], x[:, 3:4], ALU.add))
                        dve_link.link(dve, dve.reciprocal(x[:, 4:5], x[:, 2:3]))
                        done("probs_normed", dve.tensor_scalar(sc[:, n % 3, 0:w], sc[:, n % 3, 0:w], x[:, 4:5], None, ALU.mult))
                    n = i - 5
                    if 0 <= n < N:
                        q, k, bias, scale, sink, vs, ot, oh, t = units[n]
                        need(dve, "out_upper", n)
                        half, own = slice(64 * oh, 64 * oh + 64), slice(P * t, P * (t + 1))
                        o = ps[half, 4 + n % 4, 0:P]
                        done("out_copied", dve.tensor_tensor(hTl[half, ot, own].bitcast(F32R), o, hTu[half, ot, own], ALU.subtract))

            @block.gpsimd
            def _(pool):
                for i in range(N):
                    if callable(units[i][2]):
                        if i >= 2:
                            need(pool, "max", i - 2)
                        done("bias", units[i][2](pool))
        for name, t in s_at.items():
            t.n += N if name != "bias" else sum(callable(u[2]) for u in units)

    def output_stage(l):
        w0, w1 = where[f"wo{l}"], where[f"mlp{l}"]
        register_split(w0 + 1, w1)
        cols = [(4 * i, 4, [(0, 0, GW), (2, GW, GW)]) for i in range(2)]
        with nc.Block() as block:
            @block.sync
            def _(sp):
                load_until(sp, loadable(w0 + 2))

            @block.tensor
            def _(pe):
                projection(pe, f"wo{l}", cols)

            @block.scalar
            def _(act):
                for n, h in ((w0 + 1, 0), (w0 + 1, 1), (w1, 0)):
                    upper(act, w_hi, n, h)

            @block.vector
            def _(dve):
                for n, h in ((w0 + 1, 0), (w0 + 1, 1), (w1, 0)):
                    lower(dve, w_hi, w_lo, n, h)
                dve.wait_ge(ring_used, w0 + 2)
                for b in range(2):
                    x = xres[:, :, GW * b:GW * (b + 1)]
                    dve.tensor_tensor(x, x, ps[:, 2 * b:2 * b + 2, :], ALU.add)

    s_r, s_sq2, s_hh, s_c = sem("mlp_relu"), sem("mlp_squared"), sem("mlp_upper"), sem("mlp_hidden_ready")
    def mlp_stage(l, nxt):
        st = ExitStack()
        with st:
            hidT = sb(f"hiddenT{l}", [P, 4, T], stack=st)
            hidU, hidL = (sb(f"hidden{x}{l}", [P, 2, 4, T], stack=st) for x in ("U", "L"))
            junk = sb(f"mlp_junk{l}", [P, D], stack=st)
            gain = feat[:, F_MLP + 8 * l:F_MLP + 8 * (l + 1)]
            r0 = 8 * l
            w0 = where[f"mlp{l}"]
            up_at = [w0 + (0 if i == 0 else 2 * i - 1) for i in range(8)]
            down_at = [w0 + 2 * i + 2 if i < 7 else w0 + 15 for i in range(8)]
            register_split(*range(w0 + 1, w0 + 16), *([nxt] if nxt else []))
            at = s_sq.n + TT
            turn = SplitTurns(gain)
            xr = s_xnr.n + 1

            def up(pe, i):
                wu, wl, wait = split_chunk(pe, w_hi, w_lo, up_at[i])
                if i:
                    pe.wait_ge(s_r, r0 + i)
                for h in range(2):
                    wait(h)
                    for f in range(4):
                        cols = slice(P * f, P * (f + 1))
                        for k in range(4 * h, 4 * h + 4):
                            mm = product(pe, ps[:, f, 0:T], (wu[:, k, cols], wl[:, k, cols]), xT(k, slice(0, T)),
                                         k == 0, k == KT - 1)
                    mm.then_inc(ring_used if h else s_half, 1)

            def down(pe, i):
                wu, wl, wait = split_chunk(pe, w_hi, w_lo, down_at[i])
                pe.wait_ge(s_c, r0 + i + 1)
                for h in range(2):
                    wait(h)
                    for f in range(2 * h, 2 * h + 2):
                        for t in range(TT):
                            tokens = slice(P * t, P * (t + 1))
                            for b in range(2):
                                cols = slice(GW * b, GW * (b + 1))
                                mm = product(pe, ps[:, 4 + 2 * t + b, :],
                                             (hidU[:, i % 2, f, tokens].bitcast(F32R), hidL[:, i % 2, f, tokens].bitcast(F32R)),
                                             (wu[:, f, cols], wl[:, f, cols]), i == 0 and f == 0, i == 7 and f == 3)
                    mm.then_inc(ring_used if h else s_half, 1)

            with nc.Block() as block:
                @block.sync
                def _(sp):
                    load_until(sp, loadable(w0 + 16))

                @block.scalar
                def _(act):
                    norm_sums(act, junk[:, :])
                    upper(act, w_hi, w0, 1)
                    turn.act(act)
                    upper(act, w_hi, up_at[1], 0)
                    upper(act, w_hi, up_at[1], 1)
                    for i in range(8):
                        act.wait_ge(ring_used, up_at[i] + 1)
                        if i:
                            act.wait_ge(s_c, r0 + i)
                        act.activation(hidT[:, :, :], ps[:, 0:4, 0:T], ACT.Relu).then_inc(s_r, 1)
                        if 1 <= i < 7:
                            upper(act, w_hi, up_at[i + 1], 0)
                        act.wait_ge(s_sq2, r0 + i + 1)
                        if i >= 2:
                            act.wait_ge(ring_used, down_at[i - 2] + 1)
                        act.copy(hidU[:, i % 2, :, :].bitcast(F32R), hidT[:, :, :]).then_inc(s_hh, 1)
                        if 1 <= i < 7:
                            upper(act, w_hi, up_at[i + 1], 1)
                        upper(act, w_hi, down_at[i], 0)
                        upper(act, w_hi, down_at[i], 1)
                    if nxt:
                        upper(act, w_hi, nxt, 0)

                @block.vector
                def _(dve):
                    norm_scale(dve, at, mix)
                    turn.dve(dve)
                    lower(dve, w_hi, w_lo, w0, 1)
                    lower(dve, w_hi, w_lo, up_at[1], 0)
                    lower(dve, w_hi, w_lo, up_at[1], 1)
                    for i in range(8):
                        dve.wait_ge(s_r, r0 + i + 1)
                        h = hidT[:, :, :]
                        dve.tensor_tensor(h, h, h, ALU.mult).then_inc(s_sq2, 1)
                        if 1 <= i < 7:
                            lower(dve, w_hi, w_lo, up_at[i + 1], 0)
                        dve.wait_ge(s_hh, r0 + i + 1)
                        dve.tensor_tensor(hidL[:, i % 2, :, :].bitcast(F32R), h, hidU[:, i % 2, :, :], ALU.subtract).then_inc(s_c, 1)
                        if 1 <= i < 7:
                            lower(dve, w_hi, w_lo, up_at[i + 1], 1)
                        lower(dve, w_hi, w_lo, down_at[i], 0)
                        lower(dve, w_hi, w_lo, down_at[i], 1)
                    if nxt:
                        lower(dve, w_hi, w_lo, nxt, 0)
                    dve.wait_ge(ring_used, w0 + 16)
                    for t in range(TT):
                        dve.tensor_tensor(xres[:, t, :], xres[:, t, :], ps[:, 4 + 2 * t:6 + 2 * t, :].rearrange("p a b -> p (a b)"), ALU.add)

                @block.tensor
                def _(pe):
                    pe.wait_ge(s_xnr.sem, xr)
                    turn.pe(pe, mix)
                    up(pe, 0)
                    for i in range(8):
                        if i < 7:
                            up(pe, i + 1)
                        down(pe, i)

    def mla_layer():
        st = ExitStack()
        with st:
            proj = sb("mla_proj", [P, TT, MLA_IN], stack=st)
            tok = sb("mla_tok", [P, TT, MLA_H * QK], stack=st)
            v = sb("mla_v", [P, TT, MLA_H * VD], stack=st)
            qT = sb("mla_qT", [QK, MLA_H, T], stack=st)
            k_room = sb("mla_kT", [P, MLA_H, T], stack=st)
            kT = k_room[0:QK, :, :]
            qcT = sb("mla_qcT", [P, 2, T], stack=st)
            sc = sb("att_probs", [P, 3, T], stack=st)
            pT = sb("att_probsT", [P, 2, T], stack=st)
            stt = sb("att_stats", [P, 4, 8], stack=st)
            rope = sb("rope_cs", [P, 6, TT, 16], stack=st)
            cT = mix[:, :, :].rearrange("p t (k n) -> p (t k) n", n=T)
            cos, sin, ang, rnd, t1, t2 = (rope[:, i, :, :] for i in range(6))
            s_ang, s_ss, s_q, s_qT, s_qTd, s_qTa, s_cn = (sem("mla_" + n) for n in (
                "angles", "ranks_squared", "q_ready", "q_turned", "qT_even", "qT_odd", "ranks_normed"))
            s_k, s_tok = sem("mla_k_ready"), sem("mla_q_out")
            ss, vv, rstd = small[:, 8:12], small[:, 12:16], small[:, 16:20]

            def rotate(dve, x, t, n):
                x1, x2 = x[:, :, 0:16], x[:, :, 16:32]
                c, s = (y[:, t, :].unsqueeze(1).to_broadcast([P, n, 16]) for y in (cos, sin))
                w = rot_tmp[:, :, 0:n, :]
                dve.tensor_tensor(w[:, 0], x1, c, ALU.mult)
                dve.tensor_tensor(w[:, 1], x2, s, ALU.mult)
                dve.tensor_tensor(w[:, 2], x1, s, ALU.mult)
                dve_link.link(dve, dve.tensor_tensor(w[:, 3], x2, c, ALU.mult))
                dve.tensor_tensor(x1, w[:, 0], w[:, 1], ALU.subtract)
                dve_link.link(dve, dve.tensor_tensor(x2, w[:, 2], w[:, 3], ALU.add))

            rot_tmp = sc[:, :, :].rearrange("p a n -> p (a n)").rearrange("p (w h c) -> p w h c", w=4, c=16)

            def angles(dve):
                L = dve_link.link
                for t in range(TT):
                    L(dve, dve.tensor_scalar(t1[:, t, :], cst[:, C_INV:C_INV + 16], posf[:, t:t + 1], None, ALU.mult))
                L(dve, dve.tensor_scalar(t2, t1, float(1 / TWO_PI), MAGIC, ALU.mult, ALU.add))
                L(dve, dve.tensor_scalar(t2, t2, MAGIC, None, ALU.subtract))
                for part in (6.28125, 0.00193023681640625, TWO_PI - 6.28125 - 0.00193023681640625):
                    L(dve, dve.scalar_tensor_tensor(t1, t2, -float(part), t1, ALU.mult, ALU.add))
                L(dve, dve.tensor_copy(rnd, t1))
                L(dve, dve.tensor_scalar(ang, t1, float(np.pi / 2), None, ALU.add))
                L(dve, dve.tensor_scalar(t2, ang, float(np.pi), -TWO_PI, ALU.is_gt, ALU.mult))
                L(dve, dve.tensor_tensor(ang, ang, t2, ALU.add))
                for x in (ang, rnd):
                    last = dve.tensor_scalar(x, x, 3.1415925, -3.1415925, ALU.min, ALU.max)
                last.then_inc(s_ang, 1)

            f = hT[:, :, :].rearrange("p (t a) n -> p t (a n)", t=TT)
            mem_k = v[:, :, :].rearrange("p t n -> p (t n)")[:, 0:2 * TT * 256].rearrange("p (l t n) -> p l t n", l=2, t=TT)
            memT = k_room[:, 0:KT, :]
            s_x2, s_mt, s_mT, s_kd, s_kT, s_kTd = (sem(n) for n in (
                "x_second_block", "mem_turned", "memT_tile", "mem_k_out", "mem_k_turned", "mem_kT_out"))
            gain = feat[:, F_ATTN:F_ATTN + 8]
            cols = [(4 * i, 4, [(0, 0, 512), (2, 512, MLA_IN - 512)]) for i in range(2)]
            fss, fv, frstd = small[:, 0:2], small[:, 2:4], small[:, 4:6]
            at = s_sq.n
            register_split(where["mla_in"], where["mla_in"] + 1)
            turn = SplitTurns(gain)
            n1, n2 = turns.use(3), turns.use(2)
            xr = s_xnr.n + 1
            x_junk = proj[:, :, :].rearrange("p t n -> p (t n)")[:, 0:D]
            f_junk = tok[:, :, :].rearrange("p t n -> p (t n)")[:, 0:D]

            def memory_product(pe, l):
                w = chunk(pe, where[f"mem{l}"], KT)
                for k in range(KT):
                    for t in range(TT):
                        mm = pe.matmul(ps[:, t, :], memT[:, k, P * t:P * (t + 1)], w[:, k, :], start=(k == 0), stop=(k == KT - 1))
                mm.then_inc(ring_used, 1)

            def memory_out(act, l):
                act.wait_ge(ring_used, where[f"mem{l}"] + 1)
                act.copy(vm[:, l, :, :], ps[:, 0:2, 256:512])
                act.copy(mem_k[:, l, :, :], ps[:, 0:2, 0:256]).then_inc(s_kd, 1)

            with nc.Block() as block:
                @block.sync
                def _(sp):
                    load_until(sp, loadable(where["mla_in"] + 2))
                    sp.dma_start(fin_row[:, :], a["final_norm_g_2"].partition_broadcast(P)).then_inc(s_fr, 16)

                @block.scalar
                def _(act):
                    square_sums(act, [f[:, t, :] for t in range(TT)], f_junk, fss)
                    for k in range(KT):
                        act.wait_ge(s_mt, k + 1)
                        act.activation(memT[:, k, :], ps[:, 4 + k % 4, 0:T], ACT.Identity, scale=feat[:, F_MEM + k:F_MEM + k + 1]).then_inc(s_mT, 1)
                    act.wait_ge(s_x2, 1)
                    square_sums(act, [xres[:, t, :] for t in range(TT)], x_junk, fss)
                    for h in range(2):
                        upper(act, w_hi, where["mla_in"], h)
                    memory_out(act, 0)
                    turn.act(act)
                    for h in range(2):
                        upper(act, w_hi, where["mla_in"] + 1, h)
                    act.wait_ge(s_ang, 1)
                    act.activation(rope[:, 0:2, :, :], rope[:, 2:4, :, :], ACT.Sin)

                @block.vector
                def _(dve):
                    dve.wait_ge(s_sq.sem, at + TT)
                    inverse_rms(dve, dve_link, fss, fv, frstd, D, EPS)
                    for t in range(TT):
                        dve_link.link(dve, dve.scalar_tensor_tensor(f[:, t, :], f[:, t, :], frstd[:, t:t + 1], g2row[:, :], ALU.mult, ALU.mult))
                        last = dve.tensor_tensor(xres[:, t, :], xres[:, t, :], f[:, t, :], ALU.add)
                    last.then_inc(s_x2, 1)
                    norm_scale(dve, at + 2 * TT, mix)
                    for h in range(2):
                        lower(dve, w_hi, w_lo, where["mla_in"], h)
                    turn.dve(dve)
                    for h in range(2):
                        lower(dve, w_hi, w_lo, where["mla_in"] + 1, h)
                    angles(dve)
                    projection_out(dve, "mla_in", cols, proj)

                @block.tensor
                def _(pe):
                    for k in range(KT):
                        if k >= 4:
                            pe.wait_ge(s_mT, k - 3)
                        for t in range(TT):
                            mm = pe.transpose(ps[:, 4 + k % 4, P * t:P * (t + 1)], mem_tile[t][:, P * k:P * (k + 1)], ident)
                        mm.then_inc(s_mt, 1)
                    pe.wait_ge(s_mT, KT)
                    memory_product(pe, 0)
                    pe.wait_ge(s_xnr.sem, xr)
                    turn.pe(pe, mix)
                    pe.wait_ge(s_kd, 1)
                    projection(pe, "mla_in", cols)

            with nc.Block() as block:
                @block.scalar
                def _(act):
                    for t in range(TT):
                        act.activation(sc[:, 0:2, 0:192], proj[:, t, 0:Q_RANK].rearrange("p (a n) -> p a n", a=2), ACT.Square,
                                       accum_out=ss[:, t:t + 1]).then_inc(s_ss, 1)
                        act.wait_ge(s_ss, 2 * t + 1)
                        act.activation(sc[:, 0, :], proj[:, t, Q_RANK:Q_RANK + KV_RANK], ACT.Square,
                                       accum_out=ss[:, 2 + t:3 + t]).then_inc(s_ss, 1)
                        act.wait_ge(s_ss, 2 * t + 2)
                    turns.act(act, n1, cT[:, 0:3, :], 4, feat[:, F_QN:F_QN + 3])
                    turns.act(act, n2, cT[:, 3:5, :], 4, feat[:, F_KVN:F_KVN + 2])
                    memory_out(act, 1)
                    for l in range(2):
                        act.wait_ge(s_kT, l + 1)
                        act.copy(kmT[:, l, :, :], ps[:, 2 + l, :].rearrange("p (a n) -> p a n", a=2)).then_inc(s_kTd, 1)

                @block.vector
                def _(dve):
                    L = dve_link.link
                    dve.wait_ge(s_ss, 4)
                    L(dve, dve.tensor_scalar(ss[:, 0:2], ss[:, 0:2], 1.0 / Q_RANK, None, ALU.mult))
                    L(dve, dve.tensor_scalar(ss[:, 2:4], ss[:, 2:4], 1.0 / KV_RANK, None, ALU.mult))
                    inverse_rms(dve, dve_link, ss, vv, rstd, 1, EPS)
                    for t in range(TT):
                        dve.tensor_scalar(proj[:, t, 0:Q_RANK], proj[:, t, 0:Q_RANK], rstd[:, t:t + 1], None, ALU.mult)
                        last = dve.tensor_scalar(proj[:, t, Q_RANK:Q_RANK + KV_RANK], proj[:, t, Q_RANK:Q_RANK + KV_RANK],
                                                 rstd[:, 2 + t:3 + t], None, ALU.mult)
                    last.then_inc(s_cn, 1)
                    turns.dve(dve, n1, cT[:, 0:3, :], 4, feat[:, F_QN:F_QN + 3])
                    turns.dve(dve, n2, cT[:, 3:5, :], 4, feat[:, F_KVN:F_KVN + 2])

                @block.tensor
                def _(pe):
                    memory_product(pe, 1)
                    pe.wait_ge(s_cn, 1)
                    turns.pe(pe, n1, proj[:, :, 0:Q_RANK], 4)
                    turns.wait_all(pe, n1)
                    turns.pe(pe, n2, proj[:, :, Q_RANK:Q_RANK + KV_RANK], 4)
                    for l in range(2):
                        pe.wait_ge(s_kd, l + 1)
                        for i in range(2):
                            for t in range(TT):
                                mm = pe.transpose(ps[:, 2 + l, T * i + P * t:T * i + P * (t + 1)], mem_k[:, l, t, P * i:P * (i + 1)], ident)
                        mm.then_inc(s_kT, 1)

            with nc.Block() as block:
                @block.sync
                def _(sp):
                    load_until(sp, loadable(where["ukv"] + 1))

                @block.tensor
                def _(pe):
                    w = chunk(pe, where["uq"], 3)
                    for t in range(TT):
                        for k in range(3):
                            for b in range(3):
                                mm = pe.matmul(ps[:, 3 * t + b, 0:384], cT[:, k, P * t:P * (t + 1)], w[:, k, 384 * b:384 * (b + 1)],
                                               start=(k == 0), stop=(k == 2))
                    mm.then_inc(ring_used, 1)
                    w = chunk(pe, where["ukv"], 2)
                    for t in range(TT):
                        pe.wait_ge(s_tok, t + 1)
                        for k in range(2):
                            for b in range(3):
                                mm = pe.matmul(ps[:, 3 * t + b, :], cT[:, 3 + k, P * t:P * (t + 1)], w[:, k, GW * b:GW * (b + 1)],
                                               start=(k == 0), stop=(k == 1))
                    mm.then_inc(ring_used, 1)
                    pe.wait_ge(s_q, 1)
                    for h in range(MLA_H):
                        if h >= 2:
                            pe.wait_ge(s_qTa if h % 2 else s_qTd, h // 2)
                        for t in range(TT):
                            mm = pe.transpose(ps[0:QK, 6 + h % 2, P * t:P * (t + 1)], tok[:, t, QK * h:QK * (h + 1)], ident)
                        mm.then_inc(s_qT, 1)
                    pe.wait_ge(s_qTd, 6)
                    pe.wait_ge(s_qTa, 6)
                    for i in range(2):
                        for t in range(TT):
                            mm = pe.transpose(ps[:, 6, T * i + P * t:T * i + P * (t + 1)], proj[:, t, MLA_IN - 256 + P * i:MLA_IN - 256 + P * (i + 1)], ident)
                    mm.then_inc(s_qT, 1)
                    pe.wait_ge(s_k, 1)
                    pe.wait_ge(s_qTd, 7)
                    for h in range(MLA_H):
                        if h >= 2:
                            pe.wait_ge(s_qTa if h % 2 else s_qTd, 6 + h // 2 + (0 if h % 2 else 1))
                        for t in range(TT):
                            mm = pe.transpose(ps[0:QK, 6 + h % 2, P * t:P * (t + 1)], tok[:, t, QK * h:QK * (h + 1)], ident)
                        mm.then_inc(s_qT, 1)

                @block.scalar
                def _(act):
                    for r, dst in enumerate((qT, kT)):
                        for h in range(1, MLA_H, 2):
                            act.wait_ge(s_qT, 13 * r + h + 1)
                            act.copy(dst[:, h, :], ps[0:QK, 7, 0:T]).then_inc(s_qTa, 1)

                @block.vector
                def _(dve):
                    dve.wait_ge(ring_used, where["uq"] + 1)
                    for t in range(TT):
                        dve.tensor_copy(tok[:, t, :].rearrange("p (b n) -> p b n", b=3), ps[:, 3 * t:3 * t + 3, 0:384]).then_inc(s_tok, 1)
                    dve.wait_ge(s_tok, TT)
                    for t in range(TT):
                        rotate(dve, tok[:, t, :].rearrange("p (h c) -> p h c", c=QK)[:, :, NOPE:QK], t, MLA_H)
                    dve.engine_nop().then_inc(s_q, 1)
                    for t in range(TT):
                        rotate(dve, proj[:, t, Q_RANK + KV_RANK:Q_RANK + KV_RANK + ROPE].unsqueeze(1), t, 1)
                    for h in range(0, MLA_H, 2):
                        dve.wait_ge(s_qT, h + 1)
                        dve.tensor_copy(qT[:, h, :], ps[0:QK, 6, 0:T]).then_inc(s_qTd, 1)
                    dve.wait_ge(s_qT, MLA_H)
                    dve.wait_ge(ring_used, where["ukv"] + 1)
                    for t in range(TT):
                        kv = ps[:, 3 * t:3 * t + 3, :].rearrange("p b (h c) -> p (b h) c", c=NOPE + VD)
                        tk = tok[:, t, :].rearrange("p (h c) -> p h c", c=QK)
                        dve.tensor_copy(tk[:, :, 0:NOPE], kv[:, :, 0:NOPE])
                        dve.tensor_copy(v[:, t, :].rearrange("p (h c) -> p h c", c=VD), kv[:, :, NOPE:])
                        kr = proj[:, t, Q_RANK + KV_RANK:Q_RANK + KV_RANK + ROPE]
                        last = dve.tensor_copy(tk[:, :, NOPE:QK], kr.unsqueeze(1).to_broadcast([P, MLA_H, ROPE]))
                    last.then_inc(s_k, 1)
                    dve.wait_ge(s_qT, 13)
                    dve.tensor_copy(qcT[:, :, :], ps[:, 6, :].rearrange("p (a n) -> p a n", a=2)).then_inc(s_qTd, 1)
                    for h in range(0, MLA_H, 2):
                        dve.wait_ge(s_qT, 13 + h + 1)
                        dve.tensor_copy(kT[:, h, :], ps[0:QK, 6, 0:T]).then_inc(s_qTd, 1)

            units = []
            for h in range(MLA_H):
                for t in range(TT):
                    n = P * (t + 1)
                    units.append((qT[:, h, P * t:P * (t + 1)], kT[:, h, 0:n], cst[:, C_MLA + T - n:C_MLA + T], QK ** -0.5, None,
                                  [v[:, j, VD * h:VD * (h + 1)] for j in range(t + 1)], h // 2, h % 2, t))
            attention_stage(units + cross_units(0, qcT), sc, pT, stt, where["wo0"])

    def cross_units(l, qcT):
        units = []
        for h in range(CROSS_H):
            lo = 64 * (h % 2)
            for t in range(TT):
                units.append((qcT[lo:lo + 64, h // 2, P * t:P * (t + 1)], kmT[lo:lo + 64, l, h // 2, :], None, 64 ** -0.5, None,
                              [vm[:, l, j, 64 * h:64 * (h + 1)] for j in range(TT)], (MLA_H + h) // 2, h % 2, t))
        return units

    def swa_layer():
        st = ExitStack()
        with st:
            proj = sb("swa_proj", [P, TT, 3 * GW], stack=st)
            kd = sb("swa_k_twice", [P, TT, KV_H, 2, 64], stack=st)
            qT = sb("swa_qT", [P, 6, T], stack=st)
            kT = sb("swa_kT", [P, KV_H, T], stack=st)
            qcT = sb("swa_qcT", [P, 2, T], stack=st)
            dist = sb("distance", [P, TT, T], stack=st)
            bias_b = sb("distance_bias", [P, 2, T], stack=st)
            sc = sb("att_probs1", [P, 3, T], stack=st)
            pT = sb("att_probsT1", [P, 2, T], stack=st)
            stt = sb("att_stats1", [P, 4, 8], stack=st)
            normed_projection("swa_in", feat[:, F_ATTN + 8:F_ATTN + 16], [(0, 8, [(0, 0, 512)]), (0, 8, [(2, 0, 512)]), (0, 8, [(4, 0, 512)])], proj)
            s_k = sem("swa_k_doubled")
            n1, n2, n3 = turns.use(6), turns.use(4), turns.use(2)
            with nc.Block() as block:
                @block.tensor
                def _(pe):
                    turns.pe(pe, n1, proj[:, :, 0:768], 4)
                    turns.wait_all(pe, n1)
                    pe.wait_ge(s_k, 1)
                    turns.pe(pe, n2, kd[:, :, :, :, :].rearrange("p t g a c -> p t (g a c)"), 4)
                    turns.wait_all(pe, n2)
                    turns.pe(pe, n3, proj[:, :, 1280:1536], 4)

                @block.scalar
                def _(act):
                    turns.act(act, n1, qT, 4)
                    turns.act(act, n2, kT, 4)
                    turns.act(act, n3, qcT, 4)

                @block.vector
                def _(dve):
                    k = proj[:, :, 768:1024].rearrange("p t (g c) -> p t g c", c=64)
                    for i in range(2):
                        for t in range(TT):
                            last = dve.tensor_copy(kd[:, t, :, i, :], k[:, t])
                    last.then_inc(s_k, 1)
                    for t in range(TT):
                        dve_link.link(dve, dve.tensor_scalar(dist[:, t, :], posrow[:, :], posf[:, t:t + 1], -1.0, ALU.subtract, ALU.mult))
                        n = P * (t + 1)
                        dve.tensor_tensor(dist[:, t, 0:n], dist[:, t, 0:n], cst[:, C_SWA + T - n:C_SWA + T], ALU.subtract)
                    turns.dve(dve, n1, qT, 4)
                    turns.dve(dve, n2, kT, 4)
                    turns.dve(dve, n3, qcT, 4)

            scale = 64 ** -0.5

            def bias_of(h, t, n):
                slope = float(np.float32(2.0) ** np.float32(-8.0 * (h + 1.0) / SWA_H))

                def make(pool):
                    b = bias_b[:, (2 * h + t) % 2, 0:n]
                    if pool is None:
                        return b
                    return pool.tensor_scalar(b, dist[:, t, 0:n], -slope / scale, None, ALU.mult)
                return make

            units = []
            for h in range(SWA_H):
                lo, g = 64 * (h % 2), h // (SWA_H // KV_H)
                for t in range(TT):
                    n = P * (t + 1)
                    units.append((qT[lo:lo + 64, h // 2, P * t:P * (t + 1)], kT[lo:lo + 64, g, 0:n], bias_of(h, t, n), scale, sinks[:, h:h + 1],
                                  [proj[:, j, 1024 + 64 * g:1024 + 64 * (g + 1)] for j in range(t + 1)], h // 2, h % 2, t))
            attention_stage(units + cross_units(1, qcT), sc, pT, stt, where["wo1"])

    SWA_H = 12
    for l, layer in enumerate((mla_layer, swa_layer)):
        layer()
        output_stage(l)
        mlp_stage(l, None if l else where["swa_in"])

    def final_stage():
        ss, v, rstd = small[:, 0:2], small[:, 2:4], small[:, 4:6]
        at = s_sq.n + TT
        s_fin, s_out = sem("tile_final"), sem("stored")
        with nc.Block() as block:
            @block.scalar
            def _(act):
                square_sums(act, [xres[:, t, :] for t in range(TT)], mix[:, 0, :], ss)

            @block.vector
            def _(dve):
                dve.wait_ge(s_fr, 16)
                dve.wait_ge(s_sq.sem, at)
                inverse_rms(dve, dve_link, ss, v, rstd, D, EPS)
                for t in range(TT):
                    dve.scalar_tensor_tensor(xres[:, t, :], xres[:, t, :], rstd[:, t:t + 1], fin_row[:, :], ALU.mult, ALU.mult).then_inc(s_fin, 1)

            @block.sync
            def _(sp):
                for t in range(TT):
                    sp.wait_ge(s_fin, t + 1)
                    sp.dma_start(out[0, P * t:P * (t + 1), :], xres[:, t, :]).then_inc(s_out, 16)
                sp.wait_ge(s_out, 16 * TT)

    final_stage()


def kernel(**inputs):
    import concourse.bacc as _bacc
    from concourse.bass_utils import run_bass_kernel_spmd as _run

    nc = _bacc.Bacc("TRN2", target_bir_lowering=False, num_devices=1)
    arrays, args = {}, {}
    for name, value in {**inputs, **shape_tables()}.items():
        value = np.ascontiguousarray(value)
        arrays[f"in_{name}_dram"] = value
        args[name] = nc.dram_tensor(f"in_{name}_dram", value.shape, mybir.dt.from_np(value.dtype), kind="ExternalInput").ap()
    out = nc.dram_tensor("out_0_dram", (1, T, D), F32, kind="ExternalOutput").ap()
    program(nc, args, out)
    r = _run(nc, [arrays], core_ids=[0])
    return r.results[0]["out_0_dram"]
```
